# Optimizing a Trainium2 kernel written in Bass

```python
import jax, jax.numpy as jnp
from jax import lax
import numpy as np

D_MODEL = 2048
BATCH = 1
SEQ = 256
DEPTH = 2

HEAD_DIM = 128
N_HEADS = D_MODEL // HEAD_DIM
N_HEADS_A = N_HEADS // 2
N_HEADS_B = N_HEADS - N_HEADS_A
N_HEADS_C = N_HEADS
DILATED_CONFIGS = ((128, 1), (512, 4), (2048, 16))
MOBA_BLOCK = 256
MOBA_TOPK = 3
MOBA_Q_CHUNK = 16
FOX_Q_BLOCK = 128
FORGET_BIAS_MEAN = 2.0
ROT_DIM = HEAD_DIM // 4
ROPE_THETA = 500000.0
MEM_TOKENS = 256
MEM_HEADS = 4
MEM_HEAD_DIM = 128
D_FF = ((8 * D_MODEL // 3 + 255) // 256) * 256
CONV_WIDTH = 3
RMS_EPS = 1e-6
N_EVEN = (DEPTH + 1) // 2
N_ODD = DEPTH // 2

kernel_name = "hybrid_dilated_moba_fox_trunk"

def rmsnorm(x, g):
    xf = x.astype(jnp.float32)
    y = xf * lax.rsqrt(jnp.mean(xf * xf, axis=-1, keepdims=True) + RMS_EPS)
    return (y * g.astype(jnp.float32)).astype(x.dtype)

def rope_tables(positions):
    inv_freq = ROPE_THETA ** (-jnp.arange(0, ROT_DIM, 2, dtype=jnp.float32) / ROT_DIM)
    ang = positions.astype(jnp.float32)[:, None, :, None] * inv_freq
    return jnp.cos(ang), jnp.sin(ang)

def apply_partial_rope(t, cos, sin):
    half = ROT_DIM // 2
    tf = t.astype(jnp.float32)
    r1, r2 = tf[..., :half], tf[..., half:ROT_DIM]
    rot = jnp.concatenate([r1 * cos - r2 * sin, r2 * cos + r1 * sin], axis=-1)
    return jnp.concatenate([rot.astype(t.dtype), t[..., ROT_DIM:]], axis=-1)

def dilated_branch(q, k, v, dil, n_back):
    B_, H, S, E = q.shape
    L = S // dil
    Q = n_back
    nb = -(-L // Q)
    Lp = nb * Q
    scale = HEAD_DIM ** -0.5

    def split(t):
        return t.reshape(B_, H, L, dil, E).transpose(0, 1, 3, 2, 4)

    qs, ks, vs = split(q), split(k), split(v)
    pad_q = ((0, 0), (0, 0), (0, 0), (0, Lp - L), (0, 0))
    pad_k = ((0, 0), (0, 0), (0, 0), (Q, Lp - L), (0, 0))
    qb = jnp.pad(qs, pad_q).reshape(B_, H, dil, nb, Q, E)
    kp = jnp.pad(ks, pad_k).reshape(B_, H, dil, nb + 1, Q, E)
    vp = jnp.pad(vs, pad_k).reshape(B_, H, dil, nb + 1, Q, E)
    kb = jnp.concatenate([kp[:, :, :, :-1], kp[:, :, :, 1:]], axis=4)
    vb = jnp.concatenate([vp[:, :, :, :-1], vp[:, :, :, 1:]], axis=4)

    s = jnp.einsum('bhrnqe,bhrnke->bhrnqk', qb, kb).astype(jnp.float32) * scale
    qi = jnp.arange(nb)[:, None, None] * Q + jnp.arange(Q)[None, :, None]
    kj = jnp.arange(nb)[:, None, None] * Q - Q + jnp.arange(2 * Q)[None, None, :]
    dist = qi - kj
    mask = (dist >= 0) & (dist <= Q) & (kj >= 0)
    s = jnp.where(mask, s, -jnp.inf)
    m = jnp.max(s, axis=-1, keepdims=True)
    e = jnp.exp(s - m)
    den = jnp.sum(e, axis=-1)
    o = jnp.einsum('bhrnqk,bhrnke->bhrnqe', e, vb.astype(jnp.float32)) / den[..., None]
    lse = m[..., 0] + jnp.log(den)

    o = o.reshape(B_, H, dil, Lp, E)[:, :, :, :L].transpose(0, 1, 3, 2, 4).reshape(B_, H, S, E)
    lse = lse.reshape(B_, H, dil, Lp)[:, :, :, :L].transpose(0, 1, 3, 2).reshape(B_, H, S)
    return o, lse

def dilated_mixture_attention(q, k, v):
    outs, lses = [], []
    for window, dil in DILATED_CONFIGS:
        o, l = dilated_branch(q, k, v, dil, window // dil)
        outs.append(o)
        lses.append(l)
    w = jax.nn.softmax(jnp.stack(lses), axis=0)
    o = jnp.sum(w[..., None] * jnp.stack(outs), axis=0)
    return o.astype(q.dtype)

def moba_attention(q, k, v):
    B_, H, S, E = q.shape
    BS = MOBA_BLOCK
    Tc = MOBA_Q_CHUNK
    scale = HEAD_DIM ** -0.5
    Sp = -(-S // BS) * BS
    nblk = Sp // BS
    pad = ((0, 0), (0, 0), (0, Sp - S), (0, 0))
    kb = jnp.pad(k, pad).reshape(B_, H, nblk, BS, E)
    vb = jnp.pad(v, pad).reshape(B_, H, nblk, BS, E)
    kbar = jnp.mean(kb.astype(jnp.float32), axis=3)
    ksel = min(MOBA_TOPK, nblk)
    nc = S // Tc
    qc = q.reshape(B_, H, nc, Tc, E).transpose(2, 0, 1, 3, 4)
    bi = jnp.arange(B_)[:, None, None, None]
    hi = jnp.arange(H)[None, :, None, None]
    blk_ids = jnp.arange(nblk)

    def chunk(args):
        qx, c = args
        t = c * Tc + jnp.arange(Tc)
        own = (c * Tc) // BS
        gate = jnp.einsum('bhqe,bhne->bhqn', qx.astype(jnp.float32), kbar)
        gate = jnp.where(blk_ids < own, gate, -jnp.inf)
        _, idx = lax.top_k(gate, ksel)
        valid = idx < own
        kg = kb[bi, hi, idx]
        vg = vb[bi, hi, idx]
        s_sel = jnp.einsum('bhqe,bhqnke->bhqnk', qx, kg).astype(jnp.float32) * scale
        s_sel = jnp.where(valid[..., None], s_sel, -jnp.inf).reshape(B_, H, Tc, ksel * BS)
        ko = lax.dynamic_index_in_dim(kb, own, axis=2, keepdims=False)
        vo = lax.dynamic_index_in_dim(vb, own, axis=2, keepdims=False)
        s_own = jnp.einsum('bhqe,bhke->bhqk', qx, ko).astype(jnp.float32) * scale
        kpos = own * BS + jnp.arange(BS)
        s_own = jnp.where(kpos[None, :] <= t[:, None], s_own, -jnp.inf)
        p = jax.nn.softmax(jnp.concatenate([s_sel, s_own], axis=-1), axis=-1)
        p_sel = p[..., :ksel * BS].reshape(B_, H, Tc, ksel, BS)
        p_own = p[..., ksel * BS:]
        o = (jnp.einsum('bhqnk,bhqnke->bhqe', p_sel, vg.astype(jnp.float32))
             + jnp.einsum('bhqk,bhke->bhqe', p_own, vo.astype(jnp.float32)))
        return o.astype(q.dtype)

    out = lax.map(chunk, (qc, jnp.arange(nc)))
    return out.transpose(1, 2, 0, 3, 4).reshape(B_, H, S, E)

def forgetting_attention(q, k, v, logf):
    B_, H, S, E = q.shape
    QB = FOX_Q_BLOCK
    scale = HEAD_DIM ** -0.5
    c = jnp.cumsum(logf, axis=-1)
    nq = S // QB
    qb = q.reshape(B_, H, nq, QB, E).transpose(2, 0, 1, 3, 4)
    cb = c.reshape(B_, H, nq, QB).transpose(2, 0, 1, 3)
    kpos = jnp.arange(S)

    def blk(args):
        qx, cx, i = args
        tpos = i * QB + jnp.arange(QB)
        s = (jnp.einsum('bhqe,bhke->bhqk', qx, k).astype(jnp.float32) * scale
             + cx[..., None] - c[:, :, None, :])
        s = jnp.where(kpos[None, :] <= tpos[:, None], s, -jnp.inf)
        p = jax.nn.softmax(s, axis=-1)
        return jnp.einsum('bhqk,bhke->bhqe', p, v.astype(jnp.float32)).astype(q.dtype)

    out = lax.map(blk, (qb, cb, jnp.arange(nq)))
    return out.transpose(1, 2, 0, 3, 4).reshape(B_, H, S, E)

def merge_heads(o):
    B_, H, S, E = o.shape
    return o.transpose(0, 2, 1, 3).reshape(B_, S, H * E)

def even_mixer(h, w_in, w_out, cos, sin):
    B_, S, _ = h.shape
    proj = h @ w_in
    parts = proj.reshape(B_, S, 6, N_HEADS_A, HEAD_DIM).transpose(2, 0, 3, 1, 4)
    qa, ka, va, qb, kb, vb = parts[0], parts[1], parts[2], parts[3], parts[4], parts[5]
    qa, ka = apply_partial_rope(qa, cos, sin), apply_partial_rope(ka, cos, sin)
    qb, kb = apply_partial_rope(qb, cos, sin), apply_partial_rope(kb, cos, sin)
    oa = dilated_mixture_attention(qa, ka, va)
    ob = moba_attention(qb, kb, vb)
    o = jnp.concatenate([oa, ob], axis=1)
    return merge_heads(o) @ w_out

def odd_mixer(h, w_in, b_f, w_out):
    B_, S, _ = h.shape
    proj = h @ w_in
    nqkv = 3 * N_HEADS_C * HEAD_DIM
    qkv = proj[..., :nqkv].reshape(B_, S, 3, N_HEADS_C, HEAD_DIM).transpose(2, 0, 3, 1, 4)
    fg = proj[..., nqkv:].astype(jnp.float32) + b_f.astype(jnp.float32)
    logf = jax.nn.log_sigmoid(fg).transpose(0, 2, 1)
    o = forgetting_attention(qkv[0], qkv[1], qkv[2], logf)
    return merge_heads(o) @ w_out

def memory_cross_attention(h, memn, wq, wk, wv, wo):
    B_, S, _ = h.shape
    M = memn.shape[1]
    scale = MEM_HEAD_DIM ** -0.5
    q = (h @ wq).reshape(B_, S, MEM_HEADS, MEM_HEAD_DIM)
    k = (memn @ wk).reshape(B_, M, MEM_HEADS, MEM_HEAD_DIM)
    v = (memn @ wv).reshape(B_, M, MEM_HEADS, MEM_HEAD_DIM)
    s = jnp.einsum('bshe,bmhe->bhsm', q, k).astype(jnp.float32) * scale
    p = jax.nn.softmax(s, axis=-1)
    o = jnp.einsum('bhsm,bmhe->bshe', p, v.astype(jnp.float32)).astype(h.dtype)
    return o.reshape(B_, S, MEM_HEADS * MEM_HEAD_DIM) @ wo

def conv_ffn(h, w_up, conv_w, conv_b, w_down):
    S = h.shape[1]
    u = h @ w_up
    up = jnp.pad(u, ((0, 0), (CONV_WIDTH - 1, 0), (0, 0)))
    u = conv_b + conv_w[0] * up[:, 0:S] + conv_w[1] * up[:, 1:S + 1] + conv_w[2] * up[:, 2:S + 2]
    g, val = u[..., :D_FF], u[..., D_FF:]
    return (jax.nn.silu(g) * val).astype(h.dtype) @ w_down

def setup_inputs(seed: int = 0) -> dict:
    key = jax.random.key(seed)
    ks = jax.random.split(key, 24)
    f32 = jnp.float32

    def nrm(k, shape, fan_in):
        return jax.random.normal(k, shape, f32) * (fan_in ** -0.5)

    def gain(k, shape):
        return 1.0 + 0.02 * jax.random.normal(k, shape, f32)

    w_ab = (N_HEADS_A + N_HEADS_B) * HEAD_DIM
    w_c = N_HEADS_C * HEAD_DIM
    w_m = MEM_HEADS * MEM_HEAD_DIM
    x = jax.random.normal(ks[0], (BATCH, SEQ, D_MODEL), f32)
    mem = jax.random.normal(ks[1], (BATCH, MEM_TOKENS, D_MODEL), f32)
    positions = (jax.random.randint(ks[2], (BATCH, 1), 0, 1024, dtype=jnp.int32)
                 + jnp.arange(SEQ, dtype=jnp.int32)[None, :])
    return {
        "x": x,
        "mem": mem,
        "positions": positions,
        "w_in_ab": nrm(ks[3], (N_EVEN, D_MODEL, 3 * w_ab), D_MODEL),
        "w_out_ab": nrm(ks[4], (N_EVEN, w_ab, D_MODEL), w_ab),
        "w_in_c": nrm(ks[5], (N_ODD, D_MODEL, 3 * w_c + N_HEADS_C), D_MODEL),
        "b_f": FORGET_BIAS_MEAN + 0.5 * jax.random.normal(ks[6], (N_ODD, N_HEADS_C), f32),
        "w_out_c": nrm(ks[7], (N_ODD, w_c, D_MODEL), w_c),
        "g_mix_pre": gain(ks[8], (DEPTH, D_MODEL)),
        "g_mix_post": gain(ks[9], (DEPTH, D_MODEL)),
        "g_mem_kv": gain(ks[10], (DEPTH, D_MODEL)),
        "g_mem_pre": gain(ks[11], (DEPTH, D_MODEL)),
        "g_mem_post": gain(ks[12], (DEPTH, D_MODEL)),
        "w_mq": nrm(ks[13], (DEPTH, D_MODEL, w_m), D_MODEL),
        "w_mk": nrm(ks[14], (DEPTH, D_MODEL, w_m), D_MODEL),
        "w_mv": nrm(ks[15], (DEPTH, D_MODEL, w_m), D_MODEL),
        "w_mo": nrm(ks[16], (DEPTH, w_m, D_MODEL), w_m),
        "g_ffn_pre": gain(ks[17], (DEPTH, D_MODEL)),
        "g_ffn_post": gain(ks[18], (DEPTH, D_MODEL)),
        "w_up": nrm(ks[19], (DEPTH, D_MODEL, 2 * D_FF), D_MODEL),
        "conv_w": nrm(ks[20], (DEPTH, CONV_WIDTH, 2 * D_FF), CONV_WIDTH),
        "conv_b": 0.02 * jax.random.normal(ks[21], (DEPTH, 2 * D_FF), f32),
        "w_down": nrm(ks[22], (DEPTH, D_FF, D_MODEL), D_FF),
    }

def reference(x, mem, positions, w_in_ab, w_out_ab, w_in_c, b_f, w_out_c,
              g_mix_pre, g_mix_post, g_mem_kv, g_mem_pre, g_mem_post,
              w_mq, w_mk, w_mv, w_mo, g_ffn_pre, g_ffn_post,
              w_up, conv_w, conv_b, w_down):
    cos, sin = rope_tables(positions)
    for layer in range(DEPTH):
        h = rmsnorm(x, g_mix_pre[layer])
        if layer % 2 == 0:
            y = even_mixer(h, w_in_ab[layer // 2], w_out_ab[layer // 2], cos, sin)
        else:
            y = odd_mixer(h, w_in_c[layer // 2], b_f[layer // 2], w_out_c[layer // 2])
        x = x + rmsnorm(y, g_mix_post[layer])
        h = rmsnorm(x, g_mem_pre[layer])
        memn = rmsnorm(mem, g_mem_kv[layer])
        y = memory_cross_attention(h, memn, w_mq[layer], w_mk[layer], w_mv[layer], w_mo[layer])
        x = x + rmsnorm(y, g_mem_post[layer])
        h = rmsnorm(x, g_ffn_pre[layer])
        y = conv_ffn(h, w_up[layer], conv_w[layer], conv_b[layer], w_down[layer])
        x = x + rmsnorm(y, g_ffn_post[layer])
    return x


_drawn_inputs = setup_inputs


def setup_inputs(seed=0):
    import zlib

    import numpy as np

    out = dict(_drawn_inputs(seed))
    spreads = {}
    factors = {'g_mix_post': 2.809,
     'g_mem_pre': 3.643,
     'g_mem_post': 3.461,
     'g_ffn_pre': 3.033,
     'g_ffn_post': 4.301,
     'conv_b': 3.005}
    for name, (base, spread) in spreads.items():
        noise = np.random.default_rng([zlib.crc32(name.encode()), seed]).standard_normal(out[name].shape)
        drawn = base * np.exp(spread * noise) if base else spread * noise
        out[name] = __import__('jax').numpy.asarray(drawn.astype(out[name].dtype))
    for name, factor in factors.items():
        out[name] = (out[name] * factor).astype(out[name].dtype)
    return out
```

```python
from contextlib import ExitStack

import numpy as np

import concourse.bass as bass
from concourse import mybir

F32 = mybir.dt.float32
F32R = mybir.dt.float32r
I32 = mybir.dt.int32
ALU = mybir.AluOpType
ACT = mybir.ActivationFunctionType
AX = mybir.AxisListType

P = 128
D = 2048
SEQ = 256
HALF = 2
KT = D // P
HEADS = D // P
LAYERS = 2
MEM_HEADS = 4
MEM_KT = MEM_HEADS * P // P
D_FF = 5632
FF_KT = D_FF // P
N = 512
SLAB_KT = 2
RING = 4
AHEAD = 2
GS = KT // SLAB_KT
FF_GS = FF_KT // SLAB_KT
MEM_GS = MEM_KT // SLAB_KT
D_GROUPS = D // N
FF_GROUPS = D_FF // N
FF_TILES = 2 * FF_KT
CW = 3
EPS = 1e-6
SCALE = float(P) ** -0.5
MASKED = -1.0e30
GAINS = ("mix_pre", "mem_kv", "mem_pre", "ffn_pre")
ROT = P // 4
ROT_HALF = ROT // 2
W0, W1 = P, SEQ


def layer_slabs():
    at, start = 0, {}
    for name, n in (("qkv", 3 * D_GROUPS * GS), ("out", D_GROUPS * GS), ("kv", 2 * GS), ("mq", GS),
                    ("mo", D_GROUPS * MEM_GS), ("up", 2 * FF_GROUPS * GS), ("down", D_GROUPS * FF_GS)):
        start[name] = at
        at += n
    return start, at


PHASE, LAYER_SLABS = layer_slabs()
TOTAL_SLABS = LAYERS * LAYER_SLABS


def build(nc, x, mem, positions, w_in_ab, w_out_ab, w_in_c, b_f, w_out_c,
          g_mix_pre, g_mix_post, g_mem_kv, g_mem_pre, g_mem_post,
          w_mq, w_mk, w_mv, w_mo, g_ffn_pre, g_ffn_post,
          w_up, conv_w, conv_b, w_down,
          identity, inv_freq, causal_mask, dilated_mask, out):
    ctx = ExitStack()
    with ctx:
        ARENA = 212 * 1024 - 4288
        arena = ctx.enter_context(nc.sbuf_tensor("arena", [P, ARENA // 4], F32))
        base = (nc.sbuf_base - ARENA) if nc.sbuf_base > ARENA else 0
        cursor = [base]

        def place(name, shape, dtype=F32, at=None):
            size = 4 * int(np.prod(shape[1:]))
            offset = cursor[0] if at is None else at
            if at is None:
                cursor[0] += (size + 31) // 32 * 32
                assert cursor[0] <= base + ARENA, (name, cursor[0] - base, ARENA)
            return nc.alloc_sbuf_tensor_at(name, shape, dtype, offset=offset)

        x_sb = place("x_sb", [P, HALF, D])
        raw = place("raw", [P, RING, SLAB_KT, N])
        w_hi = place("w_hi", [P, RING, SLAB_KT, N], F32R)
        w_lo = place("w_lo", [P, RING, SLAB_KT, N], F32R)
        a_at = cursor[0]
        a_hi = place("a_hi", [P, KT, SEQ], F32R)
        a_lo = place("a_lo", [P, KT, SEQ], F32R)
        y_at = cursor[0]
        yg = place("yg", [P, HALF, D])
        u_gate = place("u_gate", [P, HALF, N], at=y_at)
        u_val = place("u_val", [P, HALF, N], at=y_at + 4096)
        conv_gate = place("conv_gate", [P, 4, SEQ], at=y_at + 8192)
        conv_val = place("conv_val", [P, 4, SEQ], at=y_at + 12288)
        g_post = place("g_post", [P, 2, N])
        big_at = cursor[0]
        hid_hi = place("hid_hi", [P, FF_KT, SEQ], F32R)
        hid_lo = place("hid_lo", [P, FF_KT, SEQ], F32R)
        KB = 1024
        qkT = place("qkT", [P, 2 * HEADS, SEQ], at=big_at)
        v_sb = place("v_sb", [P, HALF, D], at=big_at + 32 * KB)
        qk_stage = place("qk_stage", [P, 2, HALF, N], at=big_at + 48 * KB)
        masks = place("masks", [P, 2, W0 + W1], at=big_at + 56 * KB)
        prob = place("prob", [P, 2, W0 + W1], at=big_at + 59 * KB)
        probT = place("probT", [P, 2, W0 + W1], at=big_at + 62 * KB)
        rope_t = place("rope_t", [P, 4, HALF, 4, ROT_HALF], at=big_at + 65 * KB)
        wf_raw = place("wf_raw", [P, KT, HEADS], at=big_at + 67 * KB)
        wf_hi = place("wf_hi", [P, KT, HEADS], F32R, at=big_at + 68 * KB)
        wf_lo = place("wf_lo", [P, KT, HEADS], F32R, at=big_at + 69 * KB)
        fg_stage = place("fg_stage", [P, HALF, HEADS], at=big_at + 70 * KB)
        bf_sb = place("bf_sb", [HEADS, 1], at=big_at + 71 * KB - 64)
        fz = place("fz", [HEADS, SEQ], at=big_at + 71 * KB)
        fneg = place("fneg", [HEADS, SEQ], at=big_at + 72 * KB)
        fabs = place("fabs", [HEADS, SEQ], at=big_at + 73 * KB)
        fexp = place("fexp", [HEADS, SEQ], at=big_at + 74 * KB)
        flog = place("flog", [HEADS, SEQ], at=big_at + 75 * KB)
        fsum = place("fsum", [HEADS, SEQ], at=big_at + 76 * KB)
        fones = place("fones", [HEADS, SEQ], at=big_at + 77 * KB)
        fbias = place("fbias", [HEADS, SEQ], at=big_at + 78 * KB)
        conv_in = place("conv_in", [FF_TILES, CW + 1, P], at=big_at + 79 * KB)
        gain_in = place("gain_in", [P, P], at=big_at + 81 * KB)
        ang = place("ang", [P, 6, HALF, ROT_HALF], at=big_at + 82 * KB)
        pos_i = place("pos_i", [P, HALF], I32, at=big_at + 83 * KB)
        pos_f = place("pos_f", [P, HALF], at=big_at + 83 * KB + 32)
        invf = place("invf", [P, ROT_HALF], at=big_at + 83 * KB + 64)
        mem_sb = place("mem_sb", [P, HALF, D], at=big_at)
        m_hi = place("m_hi", [P, KT, SEQ], F32R, at=big_at + 16 * KB)
        m_lo = place("m_lo", [P, KT, SEQ], F32R, at=big_at + 32 * KB)
        mk_stage = place("mk_stage", [P, HALF, N], at=big_at + 48 * KB)
        mq_stage = place("mq_stage", [P, HALF, N], at=big_at + 52 * KB)
        mkT = place("mkT", [P, MEM_HEADS, SEQ], at=big_at + 56 * KB)
        mqT = place("mqT", [P, MEM_HEADS, SEQ], at=big_at + 60 * KB)
        mv_sb = place("mv_sb", [P, HALF, N], at=big_at + 64 * KB)
        mprob = place("mprob", [P, 2, 2 * SEQ], at=big_at + 68 * KB)
        mprobT = place("mprobT", [P, 2, 2 * SEQ], at=big_at + 72 * KB)
        junk = place("junk", [P, N], at=big_at + 86 * KB)
        junk_ffn = place("junk_ffn", [P, N], at=a_at)
        ident = place("ident", [P, P])
        gT = place("gT", [P, len(GAINS), LAYERS, KT])
        convT = place("convT", [P, CW + 1, FF_TILES])
        cos_t = place("cos_t", [P, HALF, ROT_HALF])
        sin_t = place("sin_t", [P, HALF, ROT_HALF])
        minus_half = place("minus_half", [P, HALF])
        half_pi = place("half_pi", [P, 1])
        stats = place("stats", [P, 4, 32])

        acc = ctx.enter_context(nc.psum_tensor("acc", [P, 2, HALF, N], F32))
        tp = ctx.enter_context(nc.psum_tensor("tp", [P, 2, N], F32))
        up_ = ctx.enter_context(nc.psum_tensor("aux", [P, 2, N], F32))
        aux = up_

        made = {}

        def sem(name):
            if name not in made:
                made[name] = ctx.enter_context(nc.semaphore(name))
            return made[name]

        raw_landed = [sem(f"raw_landed_{i}") for i in range(RING)]
        hi_ready = sem("hi_ready")
        lo_ready = sem("lo_ready")
        slab_used = sem("slab_used")
        x_landed = sem("x_landed")
        small_landed = sem("small_landed")
        out_stored = sem("out_stored")

        PER_LAYER = dict(
            xT=8, a_hi=16, a_lo=16, x_sq=8, xc=3, rstd=1, y_sq=8, yc=3, y_rstd=1, yg_done=4,
            g_landed_0=32, g_landed_1=32, x_new=16,
            qk_t=8, qk_ev_a=8, qk_ev_d=8, qk_st_a=8, qk_st_d=8, v_ev_a=4, v_ev_d=4,
            tables_landed=96, conv_t=1, conv_st=1, s=16, s_max=32, row_max=16, exp=32, recip=16, p=32, p_t=16,
            p_st=16, o_t=16, o_hi=16, o_lo=16,
            mem_landed=32, mem_t=8, m_hi=16, m_lo=16, mem_sq=8, mc=3, m_rstd=1, m_ev_a=3, m_ev_d=3, mqk_t=2,
            mqk_st_a=2, mqk_st_d=2, ms=4, ms_max=4, m_max=4, m_exp=8, m_recip=4, mp=8, mp_t=4, mp_st=4, mo_t=4,
            mo_hi=4, mo_lo=4,
            u_t=22, u_ev_a=22, u_ev_d=22, tap_a=88, conv_done=176, silu=11, prod=11, hid_hi=11, hid_lo=11)

        def LS(layer, name):
            return sem(name)

        def LV(layer, name, value):
            return sem(name), value + layer * PER_LAYER.get(name, 0)

        def stat(row, a, b):
            return stats[:, row, a:b]

        NORM_STEPS = KT // SLAB_KT

        SUBS = []
        for L in range(LAYERS):
            SUBS += [("mix", L), ("mem", L), ("ffn", L)]
        PRE = {"mix": 0, "mem": 2, "ffn": 3}
        POST = {"mix": g_mix_post, "mem": g_mem_post, "ffn": g_ffn_post}

        def prev_sub(sub):
            i = SUBS.index(sub)
            return SUBS[i - 1] if i else None

        def S(sub, name):
            return sem(f"{sub[0]}_{name}")

        def SV(sub, name, value):
            before = 0 if (name, sub[0]) == ("x_new", "mix") else PER_LAYER.get(name, 0)
            return sem(f"{sub[0]}_{name}"), value + sub[1] * before

        def gain(sub, kt):
            return gT[:, PRE[sub[0]], sub[1], kt:kt + 1]

        block = ctx.enter_context(nc.Block())

        @block.sync
        def _(sp):
            def slab(n, s, src):
                if not (isinstance(n, int) and n < RING):
                    sp.wait_ge(lo_ready, n - (RING - 1))
                sp.dma_start(raw[:, s], src.rearrange("(j p) n -> p j n", p=P)).then_inc(raw_landed[s], 16)

            def groups(n0, w, cols, slabs):
                for g, c0 in enumerate(cols):
                    for s in range(slabs):
                        n = n0 + g * slabs + s
                        slab(n, n % RING, w[s * SLAB_KT * P:(s + 1) * SLAB_KT * P, c0:c0 + N])

            def groups_loop(n0, w, count, col0, stride, slabs, pair=1):
                with sp.Fori(0, count) as i:
                    for g in range(pair):
                        for s in range(slabs):
                            k = g * slabs + s
                            slab(i * (pair * slabs) + (n0 + k), k % RING,
                                 w[s * SLAB_KT * P:(s + 1) * SLAB_KT * P, bass.ds(i * stride + (col0 + g * N), N)])

            def gain_chunk(sub, g):
                if g >= 2:
                    sp.wait_ge(*SV(sub, "yg_done", g - 1))
                elif prev_sub(sub):
                    sp.wait_ge(*SV(prev_sub(sub), "yg_done", D_GROUPS - 1 + g))
                row = POST[sub[0]][sub[1]:sub[1] + 1, g * N:(g + 1) * N]
                sp.dma_start(g_post[:, g % 2, :], row.to_broadcast([P, N]))\
                    .then_inc(S(sub, f"g_landed_{g % 2}"), 16)

            sp.dma_start(ident[:], identity).then_inc(small_landed, 16)
            for h in range(HALF):
                sp.dma_start(x_sb[:, h, :], x[0, h * P:(h + 1) * P, :]).then_inc(x_landed, 16)
            for a, g in enumerate((g_mix_pre, g_mem_kv, g_mem_pre, g_ffn_pre)):
                sp.dma_start(gain_in[a * LAYERS * KT:(a + 1) * LAYERS * KT, :],
                             g.rearrange("l (t p) -> (l t) p", p=P)).then_inc(small_landed, 16)
            W = [
                dict(w_in=w_in_ab[0], w_out=w_out_ab[0]),
                dict(w_in=w_in_c[0], w_out=w_out_c[0]),
            ]
            for L in range(LAYERS):
                n0 = L * LAYER_SLABS
                w_in, w_out = W[L]["w_in"], W[L]["w_out"]
                qkv = n0 + PHASE["qkv"]
                groups(qkv, w_in, [0], GS)
                if L == 0:
                    with nc.allow_non_contiguous_dma(reason="positions, once"):
                        sp.dma_start(pos_i[:], positions[0].rearrange("(h p) -> p h", p=P)).then_inc(small_landed, 16)
                    sp.dma_start(invf[:], inv_freq).then_inc(small_landed, 16)
                if L:
                    sp.wait_ge(slab_used, n0)
                small = LS(L, "tables_landed")
                sp.dma_start(masks[:, 0, :], causal_mask).then_inc(small, 16)
                sp.dma_start(masks[:, 1, :], dilated_mask).then_inc(small, 16)
                for t in range(CW):
                    sp.dma_start(conv_in[:, t, :], conv_w[L, t].rearrange("(c p) -> c p", p=P)).then_inc(small, 16)
                sp.dma_start(conv_in[:, CW, :], conv_b[L].rearrange("(c p) -> c p", p=P)).then_inc(small, 16)
                if L:
                    sp.dma_start(wf_raw[:], w_in[:, 3 * D:3 * D + HEADS].rearrange("(t p) n -> p t n", p=P))\
                        .then_inc(small, 16)
                    sp.dma_start(bf_sb[:], b_f[0].rearrange("(h o) -> h o", o=1)).then_inc(small, 16)
                groups(qkv + GS, w_in, [N], GS)
                pair = 2 * GS
                if L == 0:
                    groups(qkv + pair, w_in, [D // 2, D // 2 + N], GS)
                    groups_loop(qkv + 2 * pair, w_in, 2, 3 * D // 2, D // 2, GS, 2)
                    groups(qkv + 4 * pair, w_in, [D, D + N], GS)
                    groups(qkv + 5 * pair, w_in, [5 * D // 2, 5 * D // 2 + N], GS)
                else:
                    groups_loop(qkv + pair, w_in, 5, 2 * N, 2 * N, GS, 2)
                for g in range(D_GROUPS):
                    gain_chunk(("mix", L), g)
                    if g == 0:
                        groups(n0 + PHASE["out"], w_out, [0], GS)
                        sp.wait_ge(*LV(L, "o_hi", HEADS))
                        for h in range(HALF):
                            sp.dma_start(mem_sb[:, h, :], mem[0, h * P:(h + 1) * P, :]).then_inc(LS(L, "mem_landed"), 16)
                    else:
                        groups(n0 + PHASE["out"] + g * GS, w_out, [g * N], GS)
                groups(n0 + PHASE["kv"], w_mk[L], [0], GS)
                groups(n0 + PHASE["kv"] + GS, w_mv[L], [0], GS)
                groups(n0 + PHASE["mq"], w_mq[L], [0], GS)
                for g in range(D_GROUPS):
                    gain_chunk(("mem", L), g)
                    groups(n0 + PHASE["mo"] + g * MEM_GS, w_mo[L], [g * N], MEM_GS)
                with sp.Fori(0, FF_GROUPS) as i:
                    for g in range(2):
                        for s in range(GS):
                            k = g * GS + s
                            slab(i * (2 * GS) + (n0 + PHASE["up"] + k), k % RING,
                                 w_up[L][s * SLAB_KT * P:(s + 1) * SLAB_KT * P, bass.ds(i * N + g * D_FF, N)])
                for g in range(D_GROUPS):
                    gain_chunk(("ffn", L), g)
                    groups(n0 + PHASE["down"] + g * FF_GS, w_down[L], [g * N], FF_GS)
            last = ("end", LAYERS)
            for c in range(D_GROUPS):
                sp.wait_ge(sem("final_x"), HALF * (c + 1))
                for h in range(HALF):
                    sp.dma_start(out[0, h * P:(h + 1) * P, c * N:(c + 1) * N], x_sb[:, h, c * N:(c + 1) * N])\
                        .then_inc(out_stored, 16)
            sp.wait_ge(out_stored, 16 * HALF * D_GROUPS)

        @block.scalar
        def _(act):
            def split(n, s):
                act.wait_ge(raw_landed[s], landed(n, s))
                if not (isinstance(n, int) and n < RING):
                    act.wait_ge(slab_used, n - (RING - 1))
                act.activation(w_hi[:, s], raw[:, s], ACT.Copy).then_inc(hi_ready, 1)

            def landed(n, s):
                if isinstance(n, int):
                    return 16 * (n // RING + 1)
                return (n - s) * (16 // RING) + 16

            def ahead(n, s=None):
                if isinstance(n, int) and n + AHEAD >= TOTAL_SLABS:
                    return
                split(n + AHEAD, (n + AHEAD) % RING if s is None else (s + AHEAD) % RING)

            def norm_in(sub, s):
                if not 0 <= s < NORM_STEPS:
                    return
                act.wait_ge(*SV(sub, "xT", s + 1))
                for j in range(SLAB_KT):
                    kt = SLAB_KT * s + j
                    act.activation(a_hi[:, kt, :], tp[:, s % 2, j * SEQ:(j + 1) * SEQ], ACT.Copy,
                                   scale=gain(sub, kt)).then_inc(S(sub, "a_hi"), 1)
                if s % 2:
                    c = s // 2
                    squares(x_sb[:, :, c * N:(c + 1) * N], c, (0, 0), junk, S(sub, "x_sq"))

            squared = {"last": None}

            def squares(src, c, at, scratch, done):
                row, k = at
                for h in range(HALF):
                    if squared["last"]:
                        act.wait_ge(squared["last"], squared[squared["last"].name])
                    act.activation(scratch[:], src[:, h, :], ACT.Square,
                                   accum_out=stats[:, row, k + h * 4 + c:k + h * 4 + c + 1]).then_inc(done, 1)
                    squared["last"] = done
                    squared[done.name] = squared.get(done.name, 0) + 1

            def evac(sub_rstd, value, parity, dst, done):
                act.activation(dst, acc[:, parity, 0, :], ACT.Copy, scale=sub_rstd).then_inc(done, 1)

            split(0, 0)
            split(1, 1)
            for L in range(LAYERS):
                n0 = L * LAYER_SLABS
                mix, mm, ffn = ("mix", L), ("mem", L), ("ffn", L)
                if L == 0:
                    act.wait_ge(sem("gain_st"), 1)
                n = n0 + PHASE["qkv"]
                for s in range(GS):
                    norm_in(mix, s)
                    ahead(n + s)

                def qk_evac(G, par):
                    act.wait_ge(slab_used, G * GS + (n0 + PHASE["qkv"] + GS))
                    act.wait_ge(*SV(mix, "rstd", 1))
                    if not (isinstance(G, int) and G < 2):
                        act.wait_ge(*LV(L, "qk_t", G - 1))
                    act.activation(qk_stage[:, par, 0, :], acc[:, par, 0, :], ACT.Copy,
                                   scale=stat(1, 0, 1)).then_inc(LS(L, "qk_ev_a"), 1)

                def qk_store(G):
                    act.wait_ge(*LV(L, "qk_t", G + 1))
                    act.activation(qkT[:, bass.ds(G * 4, 2), :],
                                   tp[:, 0, :].rearrange("p (a b) -> p a b", a=2), ACT.Copy)\
                        .then_inc(LS(L, "qk_st_a"), 1)

                def qk_group(G, par, n):
                    for s in range(GS):
                        if s == 0:
                            qk_evac(G - 1, 1 - par)
                        if s == 4:
                            qk_store(G - 1)
                        ahead(n + s, s)

                if L == 0:
                    act.wait_ge(sem("angles"), 1)
                    act.activation(sin_t[:], ang[:, 4], ACT.Sin).then_inc(sem("tables"), 1)
                    act.activation(cos_t[:], ang[:, 5], ACT.Sin, bias=half_pi[:], scale=-1.0).then_inc(sem("tables"), 1)
                qk_group(1, 1, n + GS)
                with act.Fori(1, 4) as i:
                    for k in range(2):
                        qk_group(i * 2 + k, k, i * (2 * GS) + (n + k * GS))

                def v_evac(vg):
                    act.wait_ge(slab_used, n0 + PHASE["qkv"] + (9 + vg) * GS)
                    act.activation(v_sb[:, 0, vg * N:(vg + 1) * N], acc[:, vg % 2, 0, :], ACT.Copy,
                                   scale=stat(1, 0, 1)).then_inc(LS(L, "v_ev_a"), 1)

                for vg in range(4):
                    for s in range(GS):
                        if s == 0:
                            if vg == 0:
                                qk_evac(7, 1)
                            else:
                                v_evac(vg - 1)
                        if s == 4 and vg == 0:
                            qk_store(7)
                        if L and vg == 1 and s == 2:
                            act.wait_ge(*LV(L, "tables_landed", 16 * 8))
                            act.activation(wf_hi[:], wf_raw[:], ACT.Copy).then_inc(LS(L, "wf_hi"), 1)
                        ahead(n + (8 + vg) * GS + s)
                v_evac(3)
                if L:
                    act.wait_ge(*LV(L, "fg", 3))
                    act.activation(fexp[:], fabs[:], ACT.Exp, scale=-1.0).then_inc(LS(L, "fe"), 1)
                    act.wait_ge(*LV(L, "fe", 1))
                    act.activation(flog[:], fexp[:], ACT.Ln, bias=1.0).then_inc(LS(L, "fe"), 1)

                def o_hi(h):
                    act.wait_ge(*LV(L, "o_t", h + 1))
                    act.activation(a_hi[:, h, :], acc[:, h % 2, 0, 0:SEQ], ACT.Copy).then_inc(LS(L, "o_hi"), 1)

                def probs(h):
                    act.wait_ge(*LV(L, "row_max", h + 1))
                    for t, (a, b) in enumerate(((0, W0), (W0, W0 + W1))):
                        act.activation(prob[:, h % 2, a:b], prob[:, h % 2, a:b], ACT.Exp,
                                       bias=stats[:, 2, 8 * (h % 2) + 2 + t:8 * (h % 2) + 3 + t],
                                       accum_out=stats[:, 2, 8 * (h % 2) + 4 + t:8 * (h % 2) + 5 + t])\
                            .then_inc(LS(L, "exp"), 1)

                def prob_store(h):
                    act.wait_ge(*LV(L, "p_t", h + 1))
                    if h >= 2:
                        act.wait_ge(*LV(L, "o_t", h - 1))
                    act.activation(probT[:, h % 2, :], aux[:, h % 2, 0:W0 + W1], ACT.Copy).then_inc(LS(L, "p_st"), 1)

                for t in range(HEADS + 2):
                    if t < HEADS:
                        probs(t)
                    if 1 <= t <= HEADS:
                        prob_store(t - 1)
                    if t >= 2:
                        o_hi(t - 2)

                def y_squares(sub, g, n_done):
                    act.wait_ge(slab_used, n_done)
                    squares(acc[:, g % 2], g, (3, 0), junk_ffn if sub[0] == "ffn" else junk, S(sub, "y_sq"))

                def mem_hi(m):
                    act.wait_ge(*LV(L, "mem_t", m + 1))
                    for j in range(SLAB_KT):
                        kt = SLAB_KT * m + j
                        act.activation(m_hi[:, kt, :], tp[:, m % 2, j * SEQ:(j + 1) * SEQ], ACT.Copy,
                                       scale=gT[:, 1, L, kt:kt + 1]).then_inc(LS(L, "m_hi"), 1)

                n = n0 + PHASE["out"]
                for g in range(D_GROUPS):
                    for s in range(GS):
                        if g and s == 0:
                            y_squares(mix, g - 1, n + g * GS)
                        if g == 2:
                            mem_hi(s)
                        if g == 3 and s in (1, 3, 5, 7):
                            c = s // 2
                            squares(mem_sb[:, :, c * N:(c + 1) * N], c, (0, 8), junk, LS(L, "mem_sq"))
                        ahead(n + g * GS + s)
                n = n0 + PHASE["kv"]
                y_squares(mix, D_GROUPS - 1, n)

                def m_evac(k, dst, scale, done):
                    act.wait_ge(slab_used, n0 + PHASE["kv"] + (k + 1) * GS)
                    act.activation(dst[:, 0, :], acc[:, k % 2, 0, :], ACT.Copy, scale=scale).then_inc(done, 1)

                def m_store(k, dst):
                    act.wait_ge(*LV(L, "mqk_t", k + 1))
                    act.activation(dst[:, 0:2, :], aux[:, 0, :].rearrange("p (a b) -> p a b", a=2), ACT.Copy)\
                        .then_inc(LS(L, "mqk_st_a"), 1)

                for q in range(2 * GS):
                    norm_in(mm, q - 2)
                    if q == GS:
                        act.wait_ge(*LV(L, "m_rstd", 1))
                        m_evac(0, mk_stage, stat(1, 2, 3), LS(L, "m_ev_a"))
                    if q == GS + 4:
                        m_store(0, mkT)
                    ahead(n + q)
                n = n0 + PHASE["mq"]
                for s in range(GS):
                    if s == 0:
                        m_evac(1, mv_sb, stat(1, 2, 3), LS(L, "m_ev_a"))
                    ahead(n + s)
                act.wait_ge(*SV(mm, "rstd", 1))
                m_evac(2, mq_stage, stat(1, 0, 1), LS(L, "m_ev_a"))
                m_store(1, mqT)

                def m_probs(h):
                    act.wait_ge(*LV(L, "m_max", h + 1))
                    if h >= 2:
                        act.wait_ge(*LV(L, "mp_t", h - 1))
                    for t in range(HALF):
                        act.activation(mprob[:, h % 2, t * SEQ:(t + 1) * SEQ], tp[:, h % 2, t * SEQ:(t + 1) * SEQ],
                                       ACT.Exp, scale=SCALE,
                                       bias=stats[:, 2, 8 * (h % 2) + 2 + t:8 * (h % 2) + 3 + t],
                                       accum_out=stats[:, 2, 8 * (h % 2) + 4 + t:8 * (h % 2) + 5 + t])\
                            .then_inc(LS(L, "m_exp"), 1)

                def m_prob_store(h):
                    act.wait_ge(*LV(L, "mp_t", h + 1))
                    if h >= 2:
                        act.wait_ge(*LV(L, "mo_t", h - 1))
                    act.activation(mprobT[:, h % 2, :], aux[:, h % 2, :], ACT.Copy).then_inc(LS(L, "mp_st"), 1)

                def m_o_hi(h):
                    act.wait_ge(*LV(L, "mo_t", h + 1))
                    act.activation(a_hi[:, h, :], acc[:, h % 2, 0, 0:SEQ], ACT.Copy).then_inc(LS(L, "mo_hi"), 1)

                for t in range(MEM_HEADS + 2):
                    if t < MEM_HEADS:
                        m_probs(t)
                    if 1 <= t <= MEM_HEADS:
                        m_prob_store(t - 1)
                    if t >= 2:
                        m_o_hi(t - 2)
                n = n0 + PHASE["mo"]
                for g in range(D_GROUPS):
                    for s in range(MEM_GS):
                        if g and s == 0:
                            y_squares(mm, g - 1, n + g * MEM_GS)
                        ahead(n + g * MEM_GS + s)
                n = n0 + PHASE["up"]
                y_squares(mm, D_GROUPS - 1, n)

                def u_evac(k, G, dst, par):
                    act.wait_ge(slab_used, G * GS + (n0 + PHASE["up"] + GS))
                    if not (isinstance(G, int) and G < 2):
                        act.wait_ge(*LV(L, "u_t", G - 1))
                    act.activation(dst[:, 0, :], acc[:, par, 0, :], ACT.Copy, scale=stat(1, 0, 1))\
                        .then_inc(LS(L, "u_ev_a"), 1)

                def conv_tap(G, src, dst, par, i):
                    act.wait_ge(*LV(L, "u_t", G + 1))
                    if not (isinstance(i, int) and i == 0):
                        act.wait_ge(*LV(L, "hid_lo", i))
                    for j in range(4):
                        c = i * 4 + (j + par * FF_KT)
                        act.activation(dst[:, j, :], src[:, j // 2, (j % 2) * SEQ:(j % 2 + 1) * SEQ], ACT.Identity,
                                       scale=tap(CW - 1, c), bias=tap(CW, c)).then_inc(LS(L, "tap_a"), 1)

                def tap(t, c):
                    return convT[:, t, bass.ds(c, 1)]

                def silu(i):
                    act.wait_ge(*LV(L, "conv_done", i * 16 + 8))
                    act.activation(conv_gate[:], conv_gate[:], ACT.Silu).then_inc(LS(L, "silu"), 1)

                def hid_hi_part(i):
                    act.wait_ge(*LV(L, "prod", i + 1))
                    act.activation(hid_hi[:, bass.ds(i * 4, 4), :], conv_val[:], ACT.Copy).then_inc(LS(L, "hid_hi"), 1)

                def val_tail(i, q):
                    if q == 0:
                        u_evac(1, i * 2 + 1, u_val, 1)
                    if q == 3:
                        conv_tap(i * 2 + 1, aux, conv_val, 1, i)
                    if q == 5:
                        hid_hi_part(i)

                def up_pair(i, n, first):
                    for q in range(2 * GS):
                        if first:
                            norm_in(ffn, q)
                        else:
                            val_tail(i - 1, q)
                        if q == GS:
                            if first:
                                act.wait_ge(*SV(ffn, "rstd", 1))
                            u_evac(0, i * 2, u_gate, 0)
                        if q == GS + 3:
                            conv_tap(i * 2, tp, conv_gate, 0, i)
                        if q == GS + 4:
                            silu(i)
                        ahead(n + q, q)

                up_pair(0, n, True)
                with act.Fori(1, FF_GROUPS) as i:
                    up_pair(i, i * (2 * GS) + n, False)
                n = n0 + PHASE["down"]
                for g in range(D_GROUPS):
                    for s in range(FF_GS):
                        if g == 0:
                            val_tail(FF_GROUPS - 1, s)
                        if g and s == 0:
                            y_squares(ffn, g - 1, n + g * FF_GS)
                        ahead(n + g * FF_GS + s)
                y_squares(ffn, D_GROUPS - 1, n + D_GROUPS * FF_GS)

        @block.vector
        def _(dve):
            def split(n, s):
                dve.wait_ge(hi_ready, n + 1)
                dve.tensor_tensor(w_lo[:, s], raw[:, s], w_hi[:, s].bitcast(F32), ALU.subtract).then_inc(lo_ready, 1)

            def ahead(n, s=None):
                if isinstance(n, int) and n + AHEAD >= TOTAL_SLABS:
                    return
                split(n + AHEAD, (n + AHEAD) % RING if s is None else (s + AHEAD) % RING)

            def add_y(sub, s, width, x0):
                before = prev_sub(sub) if sub[0] != "end" else SUBS[-1]
                dve.wait_ge(*SV(before, "y_rstd", 1))
                dve.wait_ge(*SV(before, "yg_done", D_GROUPS))
                for h in range(HALF):
                    xs = x_sb[:, h, x0:x0 + width]
                    dve.scalar_tensor_tensor(out=xs, in0=yg[:, h, x0:x0 + width], scalar=stat(1, 4 + h, 5 + h),
                                             in1=xs, op0=ALU.mult, op1=ALU.add)\
                        .then_inc(S(sub, "x_new") if sub[0] != "end" else sem("final_x"), 1)

            def norm_in(sub, s):
                if 0 <= s < NORM_STEPS:
                    dve.wait_ge(*SV(sub, "a_hi", SLAB_KT * (s + 1)))
                    for j in range(SLAB_KT):
                        kt = SLAB_KT * s + j
                        dve.scalar_tensor_tensor(out=a_lo[:, kt, :], in0=tp[:, s % 2, j * SEQ:(j + 1) * SEQ],
                                                 scalar=gain(sub, kt), in1=a_hi[:, kt, :].bitcast(F32),
                                                 op0=ALU.mult, op1=ALU.subtract).then_inc(S(sub, "a_lo"), 1)
                if 0 <= s + 2 < NORM_STEPS and sub != SUBS[0]:
                    add_y(sub, s + 2, SLAB_KT * P, (s + 2) * SLAB_KT * P)

            def y_gain(sub, g, n_done):
                dve.wait_ge(*SV(sub, f"g_landed_{g % 2}", 16 * (g // 2 + 1)))
                for h in range(HALF):
                    dve.wait_ge(*SV(sub, "y_sq", HALF * g + h + 1))
                    i = dve.tensor_tensor(yg[:, h, g * N:(g + 1) * N], acc[:, g % 2, h, :], g_post[:, g % 2, :], ALU.mult)
                i.then_inc(S(sub, "yg_done"), 1)

            dve.memset(minus_half[:], -0.5).then_inc(sem("consts"), 1)
            dve.memset(half_pi[:], float(np.pi / 2)).then_inc(sem("consts"), 1)
            dve.wait_ge(sem("gain_t"), 1)
            dve.tensor_copy(gT[:].rearrange("p a l k -> p (a l k)"), aux[:, 0, 0:P]).then_inc(sem("gain_st"), 1)
            split(0, 0)
            split(1, 1)
            for L in range(LAYERS):
                n0 = L * LAYER_SLABS
                mix, mm, ffn = ("mix", L), ("mem", L), ("ffn", L)
                n = n0 + PHASE["qkv"]
                if L:
                    norm_in(mix, -2)
                    norm_in(mix, -1)
                else:
                    dve.wait_ge(sem("gain_st"), 1)
                for s in range(GS):
                    norm_in(mix, s)
                    ahead(n + s)

                if L == 0:
                    two_pi = 2 * np.pi
                    c1 = 6.28125
                    c2 = float(np.float32(np.floor((two_pi - c1) * 2 ** 17) / 2 ** 17))
                    c3 = float(np.float32(np.floor((two_pi - c1 - c2) * 2 ** 26) / 2 ** 26))
                    c4 = float(np.float32(two_pi - c1 - c2 - c3))
                    magic = 1.5 * 2.0 ** 23
                    step = [0]
                    chain = sem("angle_steps")

                    def then(i):
                        step[0] += 1
                        i.then_inc(chain, 1)
                        dve.wait_ge(chain, step[0])

                    dve.wait_ge(small_landed, 16 * 7)
                    then(dve.tensor_copy(pos_f[:], pos_i[:]))
                    for h in range(HALF):
                        then(dve.tensor_scalar(ang[:, 0, h, :], invf[:], pos_f[:, h:h + 1], None, ALU.mult))
                    then(dve.tensor_scalar(ang[:, 1], ang[:, 0], 1.0 / two_pi, None, ALU.mult))
                    then(dve.tensor_scalar(ang[:, 2], ang[:, 1], magic, None, ALU.add))
                    then(dve.tensor_scalar(ang[:, 1], ang[:, 2], -magic, None, ALU.add))
                    for k, (c, a, b) in enumerate(((c1, 0, 2), (c2, 2, 3), (c3, 3, 2), (c4, 2, 3))):
                        then(dve.scalar_tensor_tensor(out=ang[:, b], in0=ang[:, 1], scalar=-c, in1=ang[:, a],
                                                      op0=ALU.mult, op1=ALU.add))
                    edge = float(np.nextafter(np.float32(np.pi), np.float32(0)))
                    then(dve.tensor_scalar(ang[:, 4], ang[:, 3], edge, -edge, ALU.min, ALU.max))
                    then(dve.tensor_scalar(ang[:, 2], ang[:, 4], -1.0, None, ALU.mult))
                    dve.tensor_tensor(ang[:, 5], ang[:, 2], ang[:, 4], ALU.max).then_inc(sem("angles"), 1)

                def qk_evac(G, par):
                    dve.wait_ge(slab_used, G * GS + (n0 + PHASE["qkv"] + GS))
                    dve.wait_ge(*SV(mix, "rstd", 1))
                    if not (isinstance(G, int) and G < 2):
                        dve.wait_ge(*LV(L, "qk_t", G - 1))
                    dve.tensor_scalar(qk_stage[:, par, 1, :], acc[:, par, 1, :], stat(1, 1, 2), None, ALU.mult)\
                        .then_inc(LS(L, "qk_ev_d"), 1)
                    if L == 0:
                        if isinstance(G, int) and G == 0:
                            dve.wait_ge(sem("tables"), 2)
                        dve.wait_ge(*LV(L, "qk_ev_a", G + 1))
                        dve.wait_ge(*LV(L, "qk_ev_d", G + 1))
                        heads = qk_stage[:, par].rearrange("p h (a e) -> p h a e", e=P)
                        r1, r2 = heads[:, :, :, 0:ROT_HALF], heads[:, :, :, ROT_HALF:ROT]
                        for h in range(HALF):
                            c = cos_t[:, h:h + 1, :].to_broadcast([P, 4, ROT_HALF])
                            sn = sin_t[:, h:h + 1, :].to_broadcast([P, 4, ROT_HALF])
                            for k, (r, f) in enumerate(((r1, c), (r2, sn), (r2, c), (r1, sn))):
                                dve.tensor_tensor(rope_t[:, k, h], r[:, h], f, ALU.mult).then_inc(LS(L, "rope"), 1)
                        dve.wait_ge(*LV(L, "rope", G * 10 + 8))
                        dve.tensor_tensor(r1, rope_t[:, 0], rope_t[:, 1], ALU.subtract).then_inc(LS(L, "rope"), 1)
                        dve.tensor_tensor(r2, rope_t[:, 2], rope_t[:, 3], ALU.add).then_inc(LS(L, "rope"), 1)

                def qk_store(G):
                    dve.wait_ge(*LV(L, "qk_t", G + 1))
                    dve.tensor_copy(qkT[:, bass.ds(G * 4 + 2, 2), :], tp[:, 1, :].rearrange("p (a b) -> p a b", a=2))\
                        .then_inc(LS(L, "qk_st_d"), 1)

                def qk_group(G, par, n):
                    for s in range(GS):
                        if s == 0:
                            qk_evac(G - 1, 1 - par)
                        if s == 4:
                            qk_store(G - 1)
                        ahead(n + s, s)

                qk_group(1, 1, n + GS)
                with dve.Fori(1, 4) as i:
                    for k in range(2):
                        qk_group(i * 2 + k, k, i * (2 * GS) + (n + k * GS))

                def v_evac(vg):
                    dve.wait_ge(slab_used, n0 + PHASE["qkv"] + (9 + vg) * GS)
                    dve.tensor_scalar(v_sb[:, 1, vg * N:(vg + 1) * N], acc[:, vg % 2, 1, :], stat(1, 1, 2), None,
                                      ALU.mult).then_inc(LS(L, "v_ev_d"), 1)

                for vg in range(4):
                    for s in range(GS):
                        if s == 0:
                            if vg == 0:
                                qk_evac(7, 1)
                            else:
                                v_evac(vg - 1)
                        if s == 4 and vg == 0:
                            qk_store(7)
                        if L and vg == 1 and s == 2:
                            dve.wait_ge(*LV(L, "wf_hi", 1))
                            dve.tensor_tensor(wf_lo[:], wf_raw[:], wf_hi[:].bitcast(F32), ALU.subtract)\
                                .then_inc(LS(L, "wf_lo"), 1)
                        if L and vg == 2 and s == 4:
                            dve.wait_ge(*LV(L, "fg_mm", 1))
                            for h in range(HALF):
                                dve.tensor_scalar(fg_stage[:, h, :], aux[:, h, 0:HEADS], stat(1, h, h + 1), None,
                                                  ALU.mult).then_inc(LS(L, "fg_st"), 1)
                            dve.memset(fones[:], 1.0).then_inc(LS(L, "fg_st"), 1)
                        if L and vg == 2 and s == 6:
                            fg = LS(L, "fg")
                            dve.wait_ge(*LV(L, "fg_t", 1))
                            dve.tensor_scalar(fz[:], aux[0:HEADS, 0, 0:SEQ], bf_sb[:], None, ALU.add).then_inc(fg, 1)
                            dve.wait_ge(fg, 1)
                            dve.tensor_scalar(fneg[:], fz[:], 0.0, None, ALU.min).then_inc(fg, 1)
                            dve.wait_ge(fg, 2)
                            dve.scalar_tensor_tensor(out=fabs[:], in0=fneg[:], scalar=-2.0, in1=fz[:],
                                                     op0=ALU.mult, op1=ALU.add).then_inc(fg, 1)
                        ahead(n + (8 + vg) * GS + s)
                v_evac(3)
                if L:
                    fg = LS(L, "fg")
                    dve.wait_ge(*LV(L, "fe", 2))
                    dve.tensor_tensor(fz[:], flog[:], fneg[:], ALU.subtract).then_inc(fg, 1)
                    dve.wait_ge(fg, 4)
                    dve.tensor_tensor_scan(fsum[:], fones[:], fz[:], 0.0, ALU.mult, ALU.add).then_inc(fg, 1)
                    dve.wait_ge(fg, 5)
                    dve.tensor_scalar(fbias[:], fsum[:], 1.0 / SCALE, None, ALU.mult).then_inc(LS(L, "fbias"), 1)

                dve.wait_ge(*LV(L, "conv_t", 1))
                dve.tensor_copy(convT[:], acc[:, 1, 1, 0:(CW + 1) * FF_TILES].rearrange("p (t c) -> p t c", t=CW + 1))\
                    .then_inc(LS(L, "conv_st"), 1)

                def scores(h):
                    mask = 1 if (L == 0 and h < HEADS // 2) else 0
                    if h == 0:
                        dve.wait_ge(*LV(L, "tables_landed", 16 * (8 if L else 6)))
                    if h >= 2:
                        dve.wait_ge(*LV(L, "p_t", h - 1))
                    dve.wait_ge(*LV(L, "s", h + 1))
                    o = 8 * (h % 2)
                    for t, (a, b) in enumerate(((0, W0), (W0, W0 + W1))):
                        dve.tensor_tensor_reduce(prob[:, h % 2, a:b], tp[:, h % 2, a:b], masks[:, mask, a:b],
                                                 SCALE, 3.0 * MASKED, ALU.add, ALU.max,
                                                 stats[:, 2, o + t:o + t + 1]).then_inc(LS(L, "s_max"), 1)
                    dve.wait_ge(*LV(L, "s_max", 2 * (h + 1)))
                    dve.tensor_scalar(stats[:, 2, o + 2:o + 4], stats[:, 2, o:o + 2], -1.0, None, ALU.mult)\
                        .then_inc(LS(L, "row_max"), 1)

                def normalise(h):
                    o = 8 * (h % 2)
                    dve.wait_ge(*LV(L, "exp", 2 * (h + 1)))
                    dve.reciprocal(stats[:, 2, o + 6:o + 8], stats[:, 2, o + 4:o + 6]).then_inc(LS(L, "recip"), 1)
                    dve.wait_ge(*LV(L, "recip", h + 1))
                    for t, (a, b) in enumerate(((0, W0), (W0, W0 + W1))):
                        dve.tensor_scalar(prob[:, h % 2, a:b], prob[:, h % 2, a:b],
                                          stats[:, 2, o + 6 + t:o + 7 + t], None, ALU.mult)\
                            .then_inc(LS(L, "p"), 1)

                def o_lo(h):
                    dve.wait_ge(*LV(L, "o_hi", h + 1))
                    dve.tensor_tensor(a_lo[:, h, :], acc[:, h % 2, 0, 0:SEQ], a_hi[:, h, :].bitcast(F32),
                                      ALU.subtract).then_inc(LS(L, "o_lo"), 1)

                for t in range(HEADS + 3):
                    if t < HEADS:
                        scores(t)
                    if 1 <= t <= HEADS:
                        normalise(t - 1)
                    if t >= 3:
                        o_lo(t - 3)

                def mem_lo(m):
                    dve.wait_ge(*LV(L, "m_hi", SLAB_KT * (m + 1)))
                    for j in range(SLAB_KT):
                        kt = SLAB_KT * m + j
                        dve.scalar_tensor_tensor(out=m_lo[:, kt, :], in0=tp[:, m % 2, j * SEQ:(j + 1) * SEQ],
                                                 scalar=gT[:, 1, L, kt:kt + 1], in1=m_hi[:, kt, :].bitcast(F32),
                                                 op0=ALU.mult, op1=ALU.subtract).then_inc(LS(L, "m_lo"), 1)

                n = n0 + PHASE["out"]
                for g in range(D_GROUPS):
                    for s in range(GS):
                        if g and s == 0:
                            y_gain(mix, g - 1, n + g * GS)
                        if g == 2:
                            mem_lo(s)
                        ahead(n + g * GS + s)
                n = n0 + PHASE["kv"]
                y_gain(mix, D_GROUPS - 1, n)

                def m_evac(k, dst, scale, done):
                    dve.wait_ge(slab_used, n0 + PHASE["kv"] + (k + 1) * GS)
                    dve.tensor_scalar(dst[:, 1, :], acc[:, k % 2, 1, :], scale, None, ALU.mult).then_inc(done, 1)

                def m_store(k, dst):
                    dve.wait_ge(*LV(L, "mqk_t", k + 1))
                    dve.tensor_copy(dst[:, 2:4, :], aux[:, 1, :].rearrange("p (a b) -> p a b", a=2))\
                        .then_inc(LS(L, "mqk_st_d"), 1)

                for q in range(2 * GS):
                    norm_in(mm, q - 2)
                    if q == GS:
                        dve.wait_ge(*LV(L, "m_rstd", 1))
                        m_evac(0, mk_stage, stat(1, 3, 4), LS(L, "m_ev_d"))
                    if q == GS + 4:
                        m_store(0, mkT)
                    ahead(n + q)
                n = n0 + PHASE["mq"]
                for s in range(GS):
                    if s == 0:
                        m_evac(1, mv_sb, stat(1, 3, 4), LS(L, "m_ev_d"))
                    ahead(n + s)
                dve.wait_ge(*SV(mm, "rstd", 1))
                m_evac(2, mq_stage, stat(1, 1, 2), LS(L, "m_ev_d"))
                m_store(1, mqT)

                def m_scores(h):
                    dve.wait_ge(*LV(L, "ms", h + 1))
                    o = 8 * (h % 2)
                    dve.tensor_reduce(stats[:, 2, o:o + 2], tp[:, h % 2, :].rearrange("p (t k) -> p t k", t=HALF),
                                      AX.X, ALU.max).then_inc(LS(L, "ms_max"), 1)
                    dve.wait_ge(*LV(L, "ms_max", h + 1))
                    dve.tensor_scalar(stats[:, 2, o + 2:o + 4], stats[:, 2, o:o + 2], -SCALE, None, ALU.mult)\
                        .then_inc(LS(L, "m_max"), 1)

                def m_normalise(h):
                    o = 8 * (h % 2)
                    dve.wait_ge(*LV(L, "m_exp", 2 * (h + 1)))
                    dve.reciprocal(stats[:, 2, o + 6:o + 8], stats[:, 2, o + 4:o + 6]).then_inc(LS(L, "m_recip"), 1)
                    dve.wait_ge(*LV(L, "m_recip", h + 1))
                    for t in range(HALF):
                        pr = mprob[:, h % 2, t * SEQ:(t + 1) * SEQ]
                        dve.tensor_scalar(pr, pr, stats[:, 2, o + 6 + t:o + 7 + t], None, ALU.mult)\
                            .then_inc(LS(L, "mp"), 1)

                def m_o_lo(h):
                    dve.wait_ge(*LV(L, "mo_hi", h + 1))
                    dve.tensor_tensor(a_lo[:, h, :], acc[:, h % 2, 0, 0:SEQ], a_hi[:, h, :].bitcast(F32),
                                      ALU.subtract).then_inc(LS(L, "mo_lo"), 1)

                for t in range(MEM_HEADS + 3):
                    if t < MEM_HEADS:
                        m_scores(t)
                    if 1 <= t <= MEM_HEADS:
                        m_normalise(t - 1)
                    if t >= 3:
                        m_o_lo(t - 3)
                n = n0 + PHASE["mo"]
                for g in range(D_GROUPS):
                    for s in range(MEM_GS):
                        if g and s == 0:
                            y_gain(mm, g - 1, n + g * MEM_GS)
                        ahead(n + g * MEM_GS + s)
                n = n0 + PHASE["up"]
                y_gain(mm, D_GROUPS - 1, n)

                def u_evac(G, dst, par):
                    dve.wait_ge(slab_used, G * GS + (n0 + PHASE["up"] + GS))
                    if not (isinstance(G, int) and G < 2):
                        dve.wait_ge(*LV(L, "u_t", G - 1))
                    dve.tensor_scalar(dst[:, 1, :], acc[:, par, 1, :], stat(1, 1, 2), None, ALU.mult)\
                        .then_inc(LS(L, "u_ev_d"), 1)

                def conv_taps(G, src, dst, par, i):
                    for j in range(4):
                        c = i * 4 + (j + par * FF_KT)
                        dve.wait_ge(*LV(L, "tap_a", G * 4 + 2 * (j // 2 + 1)))
                        u = src[:, j // 2, (j % 2) * SEQ:(j % 2 + 1) * SEQ]
                        o = dst[:, j, :]
                        dve.scalar_tensor_tensor(out=o[:, 1:SEQ], in0=u[:, 0:SEQ - 1], scalar=convT[:, 1, bass.ds(c, 1)],
                                                 in1=o[:, 1:SEQ], op0=ALU.mult, op1=ALU.add)\
                            .then_inc(LS(L, "conv_done"), 1)
                    for j in range(4):
                        c = i * 4 + (j + par * FF_KT)
                        u = src[:, j // 2, (j % 2) * SEQ:(j % 2 + 1) * SEQ]
                        o = dst[:, j, :]
                        dve.wait_ge(*LV(L, "conv_done", G * 8 + (j + 1)))
                        dve.scalar_tensor_tensor(out=o[:, 2:SEQ], in0=u[:, 0:SEQ - 2], scalar=convT[:, 0, bass.ds(c, 1)],
                                                 in1=o[:, 2:SEQ], op0=ALU.mult, op1=ALU.add)\
                            .then_inc(LS(L, "conv_done"), 1)

                def val_tail(i, q):
                    if q == 0:
                        u_evac(i * 2 + 1, u_val, 1)
                    if q == 3:
                        conv_taps(i * 2 + 1, aux, conv_val, 1, i)
                    if q == 4:
                        dve.wait_ge(*LV(L, "silu", i + 1))
                        dve.wait_ge(*LV(L, "conv_done", i * 16 + 16))
                        dve.tensor_tensor(conv_val[:], conv_gate[:], conv_val[:], ALU.mult).then_inc(LS(L, "prod"), 1)
                    if q == 5:
                        dve.wait_ge(*LV(L, "hid_hi", i + 1))
                        dve.tensor_tensor(hid_lo[:, bass.ds(i * 4, 4), :], conv_val[:],
                                          hid_hi[:, bass.ds(i * 4, 4), :].bitcast(F32), ALU.subtract)\
                            .then_inc(LS(L, "hid_lo"), 1)

                def up_pair(i, n, first):
                    for q in range(2 * GS):
                        if first:
                            norm_in(ffn, q)
                        else:
                            val_tail(i - 1, q)
                        if q == GS:
                            if first:
                                dve.wait_ge(*SV(ffn, "rstd", 1))
                            u_evac(i * 2, u_gate, 0)
                        if q == GS + 3:
                            conv_taps(i * 2, tp, conv_gate, 0, i)
                        ahead(n + q, q)

                norm_in(ffn, -2)
                norm_in(ffn, -1)
                up_pair(0, n, True)
                with dve.Fori(1, FF_GROUPS) as i:
                    up_pair(i, i * (2 * GS) + n, False)
                n = n0 + PHASE["down"]
                for g in range(D_GROUPS):
                    for s in range(FF_GS):
                        if g == 0:
                            val_tail(FF_GROUPS - 1, s)
                        if g and s == 0:
                            y_gain(ffn, g - 1, n + g * FF_GS)
                        ahead(n + g * FF_GS + s)
                y_gain(ffn, D_GROUPS - 1, n + D_GROUPS * FF_GS)
            for c in range(D_GROUPS):
                add_y(("end", LAYERS), c, N, c * N)

        @block.gpsimd
        def _(pool):
            def rstd(layer, row, at, to, chain, done):
                s = stats[:, row, at:at + 8].rearrange("p (h c) -> p h c", h=HALF)
                t4 = stats[:, 1, 16:20].rearrange("p (h c) -> p h c", h=HALF)
                pool.tensor_tensor(t4, s[:, :, 0:2], s[:, :, 2:4], ALU.add).then_inc(chain, 1)
                pool.wait_ge(chain, 3 * layer + 1)
                pool.tensor_tensor(stats[:, 1, 20:22].rearrange("p (h c) -> p h c", h=HALF), t4[:, :, 0:1],
                                   t4[:, :, 1:2], ALU.add).then_inc(chain, 1)
                pool.wait_ge(chain, 3 * layer + 2)
                pool.tensor_scalar(stats[:, 1, 22:24], stats[:, 1, 20:22], 1.0 / D, EPS, ALU.mult, ALU.add)\
                    .then_inc(chain, 1)
                pool.wait_ge(chain, 3 * layer + 3)
                pool.tensor_tensor(stats[:, 1, to:to + 2], stats[:, 1, 22:24], minus_half[:], ALU.pow)\
                    .then_inc(done, 1)

            def rstd_of(sub, kind):
                if kind == "x":
                    pool.wait_ge(*SV(sub, "x_sq", HALF * 4))
                    rstd(sub[1], 0, 0, 0, S(sub, "xc"), S(sub, "rstd"))
                else:
                    pool.wait_ge(*SV(sub, "y_sq", HALF * 4))
                    rstd(sub[1], 3, 0, 4, S(sub, "yc"), S(sub, "y_rstd"))

            pool.wait_ge(sem("consts"), 2)
            for L in range(LAYERS):
                rstd_of(("mix", L), "x")
                pool.wait_ge(*LV(L, "mem_sq", HALF * 4))
                rstd(L, 0, 8, 2, LS(L, "mc"), LS(L, "m_rstd"))
                rstd_of(("mix", L), "y")
                rstd_of(("mem", L), "x")
                rstd_of(("mem", L), "y")
                rstd_of(("ffn", L), "x")
                rstd_of(("ffn", L), "y")

        @block.tensor
        def _(pe):
            def slab(n, slot, par, k0, kts, hi, lo):
                pe.wait_ge(lo_ready, n + 1)
                for j in range(SLAB_KT):
                    kt = k0 + j
                    for h in range(HALF):
                        rows = slice(h * P, (h + 1) * P)
                        o = acc[:, par, h, :]
                        pe.matmul(o, hi[:, kt, rows], w_hi[:, slot, j, :], start=(kt == 0), stop=False)
                        pe.matmul(o, hi[:, kt, rows], w_lo[:, slot, j, :], start=False, stop=False)
                        last = pe.matmul(o, lo[:, kt, rows], w_hi[:, slot, j, :], start=False, stop=(kt == kts - 1))
                last.then_inc(slab_used, 1)

            def transposes(dst, src, tiles, done):
                for j in range(tiles):
                    for h in range(HALF):
                        last = pe.transpose(dst(j, h), src(j, h), ident[:])
                if done is not None:
                    last.then_inc(done, 1)
                return last

            def norm_in(sub, s):
                if not 0 <= s < NORM_STEPS:
                    return
                if sub != SUBS[0]:
                    pe.wait_ge(*SV(sub, "x_new", HALF * (s + 1)))
                if s >= 2:
                    pe.wait_ge(*SV(sub, "a_lo", SLAB_KT * (s - 1)))
                transposes(lambda j, h: tp[:, s % 2, j * SEQ + h * P:j * SEQ + (h + 1) * P],
                           lambda j, h: x_sb[:, h, (SLAB_KT * s + j) * P:(SLAB_KT * s + j + 1) * P],
                           SLAB_KT, S(sub, "xT"))

            pe.wait_ge(small_landed, 16 * 5)
            pe.transpose(aux[:, 0, 0:P], gain_in[:], ident[:]).then_inc(sem("gain_t"), 1)
            pe.wait_ge(x_landed, 32)
            for L in range(LAYERS):
                n0 = L * LAYER_SLABS
                mix, mm, ffn = ("mix", L), ("mem", L), ("ffn", L)
                n = n0 + PHASE["qkv"]
                norm_in(mix, 0)
                norm_in(mix, 1)
                for s in range(GS):
                    if s == 0 and L:
                        pass
                    pe.wait_ge(*SV(mix, "a_lo", SLAB_KT * (s + 1)))
                    slab(n + s, (n + s) % RING, 0, SLAB_KT * s, KT, a_hi, a_lo)
                    norm_in(mix, s + 2)

                def qk_free(G):
                    if not (isinstance(G, int) and G < 2):
                        pe.wait_ge(*LV(L, "qk_ev_a", G - 1))
                        pe.wait_ge(*LV(L, "qk_ev_d", G - 1))

                def qk_turn(G, par):
                    if L == 0:
                        pe.wait_ge(*LV(L, "rope", G * 10 + 10))
                    else:
                        pe.wait_ge(*LV(L, "qk_ev_a", G + 1))
                        pe.wait_ge(*LV(L, "qk_ev_d", G + 1))
                    if not (isinstance(G, int) and G == 0):
                        pe.wait_ge(*LV(L, "qk_st_a", G))
                        pe.wait_ge(*LV(L, "qk_st_d", G))
                    transposes(lambda j, h: tp[:, j // 2, (j % 2) * SEQ + h * P:(j % 2) * SEQ + (h + 1) * P],
                               lambda j, h: qk_stage[:, par, h, j * P:(j + 1) * P], 4, LS(L, "qk_t"))

                def qk_group(G, par, n):
                    qk_free(G)
                    for s in range(GS):
                        if s == 3:
                            qk_turn(G - 1, 1 - par)
                        slab(n + s, s % RING, par, SLAB_KT * s, KT, a_hi, a_lo)

                qk_group(1, 1, n + GS)
                with pe.Fori(1, 4) as i:
                    for k in range(2):
                        qk_group(i * 2 + k, k, i * (2 * GS) + (n + k * GS))
                for vg in range(4):
                    if vg < 2:
                        qk_free(8 + vg)
                    else:
                        pe.wait_ge(*LV(L, "v_ev_a", vg - 1))
                        pe.wait_ge(*LV(L, "v_ev_d", vg - 1))
                    for s in range(GS):
                        if s == 3 and vg == 0:
                            qk_turn(7, 1)
                        if L and vg == 2 and s == 2:
                            pe.wait_ge(*LV(L, "wf_lo", 1))
                            for h in range(HALF):
                                rows = slice(h * P, (h + 1) * P)
                                for kt in range(KT):
                                    o = aux[:, h, 0:HEADS]
                                    pe.matmul(o, a_hi[:, kt, rows], wf_hi[:, kt, :], start=(kt == 0), stop=False)
                                    pe.matmul(o, a_hi[:, kt, rows], wf_lo[:, kt, :], start=False, stop=False)
                                    last = pe.matmul(o, a_lo[:, kt, rows], wf_hi[:, kt, :], start=False,
                                                     stop=(kt == KT - 1))
                            last.then_inc(LS(L, "fg_mm"), 1)
                        if L and vg == 2 and s == 5:
                            pe.wait_ge(*LV(L, "fg_st", 2))
                            for h in range(HALF):
                                last = pe.transpose(aux[0:HEADS, 0, h * P:(h + 1) * P], fg_stage[:, h, :], ident[:])
                            last.then_inc(LS(L, "fg_t"), 1)
                        slab(n + (8 + vg) * GS + s, s % RING, vg % 2, SLAB_KT * s, KT, a_hi, a_lo)

                pe.wait_ge(*LV(L, "v_ev_d", 4))
                pe.wait_ge(*LV(L, "tables_landed", 16 * (8 if L else 6)))
                for t in range(CW + 1):
                    last = pe.transpose(acc[:, 1, 1, t * FF_TILES:(t + 1) * FF_TILES], conv_in[:, t, :],
                                        ident[0:FF_TILES, 0:FF_TILES])
                last.then_inc(LS(L, "conv_t"), 1)

                def slots(h):
                    if L:
                        return h, HEADS + h
                    q = (h // 8) * 16 + h % 8
                    return q, q + 8

                def scores(h):
                    q, k = slots(h)
                    if h == 0:
                        pe.wait_ge(*LV(L, "qk_st_a", 8))
                        pe.wait_ge(*LV(L, "qk_st_d", 8))
                        if L:
                            pe.wait_ge(*LV(L, "fbias", 1))
                    if h >= 2:
                        pe.wait_ge(*LV(L, "s_max", 2 * (h - 1)))
                    for t, (a, b) in enumerate(((0, W0), (W0, W0 + W1))):
                        o = tp[:, h % 2, a:b]
                        last = pe.matmul(o, qkT[:, q, t * P:(t + 1) * P], qkT[:, k, 0:b - a], start=True, stop=(L == 0))
                        if L:
                            last = pe.matmul(o, ident[0:HEADS, h:h + 1].to_broadcast([HEADS, P]), fbias[:, 0:b - a],
                                             start=False, stop=True)
                    last.then_inc(LS(L, "s"), 1)

                def turn_probs(h):
                    pe.wait_ge(*LV(L, "p", 2 * (h + 1)))
                    if h >= 2:
                        pe.wait_ge(*LV(L, "p_st", h - 1))
                    for k in range(3):
                        last = pe.transpose(aux[:, h % 2, k * P:(k + 1) * P], prob[:, h % 2, k * P:(k + 1) * P], ident[:])
                    last.then_inc(LS(L, "p_t"), 1)

                def values(h):
                    pe.wait_ge(*LV(L, "p_st", h + 1))
                    if h == 0:
                        pe.wait_ge(*LV(L, "v_ev_a", 4))
                    if h >= 2:
                        pe.wait_ge(*LV(L, "o_lo", h - 1))
                    o = acc[:, h % 2, 0, 0:SEQ]
                    cols = slice(h * P, (h + 1) * P)
                    pe.matmul(o, v_sb[:, 0, cols], probT[:, h % 2, 0:SEQ], start=True, stop=False)
                    pe.matmul(o[:, P:SEQ], v_sb[:, 1, cols], probT[:, h % 2, SEQ:SEQ + P], start=False, stop=True)\
                        .then_inc(LS(L, "o_t"), 1)

                scores(0)
                scores(1)
                for t in range(HEADS + 1):
                    if t < HEADS:
                        turn_probs(t)
                    if t + 2 < HEADS:
                        scores(t + 2)
                    if t >= 1:
                        values(t - 1)

                def y_free(sub, g):
                    if g >= 2:
                        pe.wait_ge(*SV(sub, "y_sq", HALF * (g - 1)))
                        pe.wait_ge(*SV(sub, "yg_done", g - 1))

                n = n0 + PHASE["out"]
                for g in range(D_GROUPS):
                    y_free(mix, g)
                    if g == 1:
                        pe.wait_ge(*LV(L, "conv_st", 1))
                    for s in range(GS):
                        if g == 0:
                            pe.wait_ge(*LV(L, "o_lo", SLAB_KT * (s + 1) if s < GS - 1 else HEADS))
                            if s == 0:
                                pe.wait_ge(*LV(L, "o_lo", HEADS))
                        slab(n + g * GS + s, (n + s) % RING, g % 2, SLAB_KT * s, KT, a_hi, a_lo)
                        m = (g - 2) * GS + s + 1
                        if 0 <= m < NORM_STEPS:
                            if m == 0:
                                pe.wait_ge(*LV(L, "mem_landed", 32))
                            if m >= 2:
                                pe.wait_ge(*LV(L, "m_lo", SLAB_KT * (m - 1)))
                            transposes(lambda j, h: tp[:, m % 2, j * SEQ + h * P:j * SEQ + (h + 1) * P],
                                       lambda j, h: mem_sb[:, h, (SLAB_KT * m + j) * P:(SLAB_KT * m + j + 1) * P],
                                       SLAB_KT, LS(L, "mem_t"))
                n = n0 + PHASE["kv"]

                def m_turn(k, src):
                    pe.wait_ge(*LV(L, "m_ev_a", 1 + 2 * k))
                    pe.wait_ge(*LV(L, "m_ev_d", 1 + 2 * k))
                    if k:
                        pe.wait_ge(*LV(L, "mqk_st_a", 1))
                        pe.wait_ge(*LV(L, "mqk_st_d", 1))
                    transposes(lambda j, h: aux[:, j // 2, (j % 2) * SEQ + h * P:(j % 2) * SEQ + (h + 1) * P],
                               lambda j, h: src[:, h, j * P:(j + 1) * P], 4, LS(L, "mqk_t"))

                for q in range(2 * GS):
                    if q % GS == 0:
                        g = D_GROUPS + q // GS
                        y_free(mix, g)
                    if q == 0:
                        pe.wait_ge(*LV(L, "m_lo", KT))
                    if q == GS + 3:
                        m_turn(0, mk_stage)
                    slab(n + q, q % RING, q // GS, SLAB_KT * (q % GS), KT, m_hi, m_lo)
                    norm_in(mm, q - 1)
                n = n0 + PHASE["mq"]
                pe.wait_ge(*SV(mm, "a_lo", KT))
                for s in range(GS):
                    slab(n + s, s % RING, 0, SLAB_KT * s, KT, a_hi, a_lo)
                m_turn(1, mq_stage)

                def m_scores(h):
                    if h == 0:
                        for k in ("mqk_st_a", "mqk_st_d"):
                            pe.wait_ge(*LV(L, k, 2))
                        pe.wait_ge(*SV(mm, "a_lo", KT))
                    if h >= 2:
                        pe.wait_ge(*LV(L, "m_exp", 2 * (h - 1)))
                    for t in range(HALF):
                        last = pe.matmul(tp[:, h % 2, t * SEQ:(t + 1) * SEQ], mqT[:, h, t * P:(t + 1) * P], mkT[:, h, :],
                                         start=True, stop=True)
                    last.then_inc(LS(L, "ms"), 1)

                def m_turn_probs(h):
                    pe.wait_ge(*LV(L, "mp", 2 * (h + 1)))
                    if h >= 2:
                        pe.wait_ge(*LV(L, "mp_st", h - 1))
                    for t in range(HALF):
                        for b in range(HALF):
                            last = pe.transpose(aux[:, h % 2, b * SEQ + t * P:b * SEQ + (t + 1) * P],
                                                mprob[:, h % 2, t * SEQ + b * P:t * SEQ + (b + 1) * P], ident[:])
                    last.then_inc(LS(L, "mp_t"), 1)

                def m_values(h):
                    pe.wait_ge(*LV(L, "mp_st", h + 1))
                    if h == 0:
                        pe.wait_ge(*LV(L, "m_ev_a", 3))
                        pe.wait_ge(*LV(L, "m_ev_d", 3))
                    if h >= 2:
                        pe.wait_ge(*LV(L, "mo_lo", h - 1))
                    o = acc[:, h % 2, 0, 0:SEQ]
                    for b in range(HALF):
                        last = pe.matmul(o, mv_sb[:, b, h * P:(h + 1) * P], mprobT[:, h % 2, b * SEQ:(b + 1) * SEQ],
                                         start=(b == 0), stop=(b == 1))
                    last.then_inc(LS(L, "mo_t"), 1)

                m_scores(0)
                m_scores(1)
                for t in range(MEM_HEADS + 1):
                    if t < MEM_HEADS:
                        m_turn_probs(t)
                    if t + 2 < MEM_HEADS:
                        m_scores(t + 2)
                    if t >= 1:
                        m_values(t - 1)
                n = n0 + PHASE["mo"]
                pe.wait_ge(*LV(L, "mo_lo", MEM_HEADS))
                for g in range(D_GROUPS):
                    y_free(mm, g)
                    for s in range(MEM_GS):
                        k = g * MEM_GS + s
                        slab(n + k, k % RING, g % 2, SLAB_KT * s, MEM_KT, a_hi, a_lo)
                n = n0 + PHASE["up"]

                def u_free(G):
                    if not (isinstance(G, int) and G < 2):
                        pe.wait_ge(*LV(L, "u_ev_a", G - 1))
                        pe.wait_ge(*LV(L, "u_ev_d", G - 1))

                def u_turn(G, src, dst):
                    pe.wait_ge(*LV(L, "u_ev_a", G + 1))
                    pe.wait_ge(*LV(L, "u_ev_d", G + 1))
                    if not (isinstance(G, int) and G < 2):
                        pe.wait_ge(*LV(L, "conv_done", (G - 1) * 8))
                    transposes(lambda j, h: dst[:, j // 2, (j % 2) * SEQ + h * P:(j % 2) * SEQ + (h + 1) * P],
                               lambda j, h: src[:, h, j * P:(j + 1) * P], 4, LS(L, "u_t"))

                def up_pair(i, n, first):
                    for q in range(2 * GS):
                        if q % GS == 0:
                            u_free(i * 2 + q // GS)
                            if first and q:
                                y_free(mm, D_GROUPS + 1)
                        if first and q < GS:
                            pe.wait_ge(*SV(ffn, "a_lo", SLAB_KT * (q + 1)))
                        if q == 2 and not first:
                            u_turn(i * 2 - 1, u_val, aux)
                        if q == GS + 2:
                            u_turn(i * 2, u_gate, tp)
                        slab(n + q, q % RING, q // GS, SLAB_KT * (q % GS), KT, a_hi, a_lo)
                        if first:
                            norm_in(ffn, q + 2)

                norm_in(ffn, 0)
                norm_in(ffn, 1)
                up_pair(0, n, True)
                with pe.Fori(1, FF_GROUPS) as i:
                    up_pair(i, i * (2 * GS) + n, False)
                n = n0 + PHASE["down"]
                for g in range(D_GROUPS):
                    if g < 2:
                        u_free(2 * FF_GROUPS + g)
                    y_free(ffn, g)
                    for s in range(FF_GS):
                        if g == 0 and s == 2:
                            u_turn(2 * FF_GROUPS - 1, u_val, aux)
                        if g == 0:
                            pe.wait_ge(*LV(L, "hid_lo", (SLAB_KT * s) // 4 + 1))
                        k = g * FF_GS + s
                        slab(n + k, k % RING, g % 2, SLAB_KT * s, FF_KT, hid_hi, hid_lo)


def tables():
    inv_freq = np.float32(500000.0) ** (-np.arange(0, ROT, 2, dtype=np.float32) / np.float32(ROT))
    q = np.arange(SEQ)[:, None]
    k = np.arange(SEQ)[None, :]
    dist = q - k
    causal = dist >= 0
    seen = np.zeros((SEQ, SEQ), np.int64)
    for window, dil in ((128, 1), (512, 4), (2048, 16)):
        seen += causal & (dist % dil == 0) & (dist <= window)
    more = np.where(seen > 0, np.log(np.maximum(seen, 1)) / SCALE, MASKED)
    plain = np.where(causal, 0.0, MASKED)

    def pair(m):
        return np.concatenate([m[:P, :W0], m[P:, :W1]], axis=1).astype(np.float32)

    return (np.eye(P, dtype=np.float32), np.tile(inv_freq.astype(np.float32), (P, 1)), pair(plain), pair(more))


_INS = ["x", "mem", "positions", "w_in_ab", "w_out_ab", "w_in_c", "b_f", "w_out_c",
        "g_mix_pre", "g_mix_post", "g_mem_kv", "g_mem_pre", "g_mem_post",
        "w_mq", "w_mk", "w_mv", "w_mo", "g_ffn_pre", "g_ffn_post",
        "w_up", "conv_w", "conv_b", "w_down"]


def kernel(**inputs):
    import concourse.bacc as _bacc
    from concourse.bass_utils import run_bass_kernel_spmd as _run

    nc = _bacc.Bacc("TRN2", target_bir_lowering=False, num_devices=1)
    arrays, args = {}, []
    named = [(n, np.ascontiguousarray(inputs[n])) for n in _INS]
    named += list(zip(("identity", "inv_freq", "causal_mask", "dilated_mask"), tables()))
    for name, a in named:
        arrays[f"in_{name}"] = a
        args.append(nc.dram_tensor(f"in_{name}", a.shape, mybir.dt.from_np(a.dtype), kind="ExternalInput").ap())
    out = nc.dram_tensor("out_0", (1, SEQ, D), F32, kind="ExternalOutput").ap()
    build(nc, *args, out)
    r = _run(nc, [arrays], core_ids=[0])
    return r.results[0]["out_0"]
```

```python
from contextlib import ExitStack

import numpy as np

import concourse.bass as bass
from concourse import mybir

F32 = mybir.dt.float32
F32R = mybir.dt.float32r
I32 = mybir.dt.int32
ALU = mybir.AluOpType
ACT = mybir.ActivationFunctionType
AX = mybir.AxisListType

P = 128
D = 2048
SEQ = 256
HALF = 2
KT = D // P
HEADS = D // P
LAYERS = 2
MEM_HEADS = 4
MEM_KT = MEM_HEADS * P // P
D_FF = 5632
FF_KT = D_FF // P
N = 512
SLAB_KT = 2
RING = 4
AHEAD = 2
TAIL = 4
LEAD = 3
GS = KT // SLAB_KT
FF_GS = FF_KT // SLAB_KT
MEM_GS = MEM_KT // SLAB_KT
D_GROUPS = D // N
FF_GROUPS = D_FF // N
FF_TILES = 2 * FF_KT
CW = 3
EPS = 1e-6
SCALE = float(P) ** -0.5
MASKED = -1.0e30
X_PIECES = ((0, 256), (256, 512), (512, 1024), (1024, 1536), (1536, D))
GAINS = ("mix_pre", "mem_kv", "mem_pre", "ffn_pre")
ROT = P // 4
ROT_HALF = ROT // 2
W0, W1 = P, SEQ


def layer_slabs():
    at, start = 0, {}
    for name, n in (("qkv", 3 * D_GROUPS * GS), ("mk", GS), ("out", D_GROUPS * GS), ("mq", GS),
                    ("mv", GS), ("mo", D_GROUPS * MEM_GS), ("up", 2 * FF_GROUPS * GS), ("down", D_GROUPS * FF_GS)):
        start[name] = at
        at += n
    return start, at


PHASE, LAYER_SLABS = layer_slabs()
TOTAL_SLABS = LAYERS * LAYER_SLABS


def build(nc, x, mem, positions, w_in_ab, w_out_ab, w_in_c, b_f, w_out_c,
          g_mix_pre, g_mix_post, g_mem_kv, g_mem_pre, g_mem_post,
          w_mq, w_mk, w_mv, w_mo, g_ffn_pre, g_ffn_post,
          w_up, conv_w, conv_b, w_down,
          identity, inv_freq, causal_mask, dilated_mask, out):
    ctx = ExitStack()
    with ctx:
        ARENA = 212 * 1024 - 4288
        arena = ctx.enter_context(nc.sbuf_tensor("arena", [P, ARENA // 4], F32))
        base = (nc.sbuf_base - ARENA) if nc.sbuf_base > ARENA else 0
        cursor = [base]

        def place(name, shape, dtype=F32, at=None):
            size = 4 * int(np.prod(shape[1:]))
            offset = cursor[0] if at is None else at
            if at is None:
                cursor[0] += (size + 31) // 32 * 32
                assert cursor[0] <= base + ARENA, (name, cursor[0] - base, ARENA)
            return nc.alloc_sbuf_tensor_at(name, shape, dtype, offset=offset)

        x_sb = place("x_sb", [P, HALF, D])
        raw = place("raw", [P, RING, SLAB_KT, N])
        w_hi = place("w_hi", [P, RING, SLAB_KT, N], F32R)
        w_lo = place("w_lo", [P, RING, SLAB_KT, N], F32R)
        a_at = cursor[0]
        a_hi = place("a_hi", [P, KT, SEQ], F32R)
        a_lo = place("a_lo", [P, KT, SEQ], F32R)
        y_at = cursor[0]
        yg = place("yg", [P, HALF, D])
        u_gate = place("u_gate", [P, HALF, N], at=y_at)
        u_val = place("u_val", [P, HALF, N], at=y_at + 4096)
        conv_gate = place("conv_gate", [P, 4, SEQ], at=y_at + 8192)
        conv_val = place("conv_val", [P, 4, SEQ], at=y_at + 12288)
        g_post = place("g_post", [P, 2, N])
        big_at = cursor[0]
        hid_hi = place("hid_hi", [P, FF_KT, SEQ], F32R)
        hid_lo = place("hid_lo", [P, FF_KT, SEQ], F32R)
        KB = 1024
        qkT = place("qkT", [P, 2 * HEADS, SEQ], at=big_at)
        v_sb = place("v_sb", [P, HALF, D], at=big_at + 32 * KB)
        m_hi = place("m_hi", [P, KT, SEQ], F32R, at=big_at + 48 * KB)
        m_lo = place("m_lo", [P, KT, SEQ], F32R, at=big_at + 64 * KB)
        masks = place("masks", [P, 2, W0 + W1], at=big_at + 80 * KB)
        conv_in = place("conv_in", [FF_TILES, CW + 1, P], at=big_at + 83 * KB)
        fb = place("fb", [P // 2, SEQ], F32R, at=big_at + 85 * KB)
        mkT = place("mkT", [P, MEM_HEADS, SEQ], at=big_at)
        mqT = place("mqT", [P, MEM_HEADS, SEQ], at=big_at + 4 * KB)
        mv_sb = place("mv_sb", [P, HALF, N], at=big_at + 8 * KB)
        mq_stage = place("mq_stage", [P, HALF, N], at=big_at + 12 * KB)
        mprob = place("mprob", [P, MEM_HEADS, 2 * SEQ], at=big_at + 16 * KB)
        mprobT = place("mprobT", [P, MEM_HEADS, 2 * SEQ], at=big_at + 24 * KB)
        qk_stage = place("qk_stage", [P, 2, HALF, N], at=y_at)
        rope_t = place("rope_t", [P, 4, HALF, 4, ROT_HALF], at=y_at + 8 * KB)
        gain_in = place("gain_in", [P, P], at=y_at + 10 * KB)
        ang = place("ang", [P, 6, HALF, ROT_HALF], at=y_at + 10 * KB + 512)
        pos_i = place("pos_i", [P, HALF], I32, at=y_at + 11 * KB + 512)
        pos_f = place("pos_f", [P, HALF], at=y_at + 11 * KB + 544)
        invf = place("invf", [P, ROT_HALF], at=y_at + 11 * KB + 576)
        mem_in = place("mem_in", [P, HALF, N], at=y_at + 12 * KB)
        mk_stage = place("mk_stage", [P, HALF, N], at=y_at + 12 * KB)
        prob = place("prob", [P, 4, W0 + W1], at=y_at)
        probT = place("probT", [P, 2, W0 + W1], at=y_at + 6 * KB)
        wf_raw = place("wf_raw", [P, KT, HEADS], at=y_at)
        wf_hi = place("wf_hi", [P, KT, HEADS], F32R, at=y_at + 1 * KB)
        wf_lo = place("wf_lo", [P, KT, HEADS], F32R, at=y_at + 2 * KB)
        fz = place("fz", [HEADS, SEQ], at=y_at + 3 * KB)
        fneg = place("fneg", [HEADS, SEQ], at=y_at + 4 * KB)
        fabs = place("fabs", [HEADS, SEQ], at=y_at + 5 * KB)
        fones = place("fones", [HEADS, SEQ], at=y_at + 6 * KB)
        fbias = place("fbias", [HEADS, SEQ], at=y_at + 7 * KB)
        bf_sb = place("bf_sb", [HEADS, 1], at=y_at + 11 * KB + 256)
        junk = place("junk", [P, N], at=big_at + 86 * KB)
        junk_ffn = place("junk_ffn", [P, N], at=a_at)
        ident = place("ident", [P, P])
        gT = place("gT", [P, len(GAINS), LAYERS, KT])
        convT = place("convT", [P, CW + 1, FF_TILES])
        cos_t = place("cos_t", [P, HALF, ROT_HALF])
        sin_t = place("sin_t", [P, HALF, ROT_HALF])
        sel = place("sel", [P // 2, HEADS], F32R)
        minus_half = place("minus_half", [P, HALF])
        half_pi = place("half_pi", [P, 1])
        stats = place("stats", [P, 4, 32])

        acc = ctx.enter_context(nc.psum_tensor("acc", [P, 2, HALF, N], F32))
        tp = ctx.enter_context(nc.psum_tensor("tp", [P, 2, N], F32))
        aux = ctx.enter_context(nc.psum_tensor("aux", [P, 2, N], F32))

        made = {}

        def sem(name):
            if name not in made:
                made[name] = ctx.enter_context(nc.semaphore(name))
            return made[name]

        raw_landed = [sem(f"raw_landed_{i}") for i in range(RING)]
        hi_ready = sem("hi_ready")
        lo_ready = sem("lo_ready")
        slab_used = sem("slab_used")
        x_landed = [sem(f"x_landed_{c}") for c in range(len(X_PIECES))]
        small_landed = sem("small_landed")
        out_stored = sem("out_stored")

        PER_LAYER = dict(
            xT=11, a_hi=22, a_lo=22, x_sq=8, xc=4, rstd=1, y_half=4, y_sq=8, yc=6, y_rstd=2, yg_done=8,
            g_landed_0=32, g_landed_1=32, x_new=16,
            qk_t=8, qk_ev_a=8, qk_ev_d=8, qk_st_a=8, qk_st_d=8, v_ev_a=4, v_ev_d=4,
            tables_landed=96, conv_t=1, conv_st=1, s=16, s_max=32, row_max=16, exp=32, recip=16, p=32, p_t=16,
            p_st=16, o_t=16, o_hi=16, o_lo=16,
            mem_landed=64, mem_t=8, m_hi=16, m_lo=16, mem_sq=8, mc=4, m_rstd=1, m_ev_a=3, m_ev_d=3, mqk_t=2,
            mqk_st_a=2, mqk_st_d=2, ms=4, ms_max=4, m_max=4, m_exp=8, m_recip=4, mp=8, mp_t=4, mp_st=4, mo_t=4,
            mo_hi=4, mo_lo=4, mv_half=1,
            u_t=22, u_ev_a=22, u_ev_d=22, tap_a=88, conv_done=176, silu=11, prod=11, hid_hi=11, hid_lo=11)

        def LS(layer, name):
            return sem(name)

        def LV(layer, name, value):
            return sem(name), value + layer * PER_LAYER.get(name, 0)

        def stat(row, a, b):
            return stats[:, row, a:b]

        NORM_STEPS = KT // SLAB_KT
        ITEMS = NORM_STEPS + LEAD

        def item(sub, i):
            if i >= 2 * LEAD:
                return i - LEAD, (0, 1)
            return (i // 2, (i % 2,)) if sub == SUBS[0] else (i % LEAD, (i // LEAD,))

        def item_bank(i):
            return (tp[:, 0], aux[:, 0], tp[:, 1], aux[:, 1])[i % 4]

        def item_tile(sub, i, j):
            s, hs = item(sub, i)
            width = len(hs) * P
            return item_bank(i)[:, j * width:(j + 1) * width], SLAB_KT * s + j, slice(hs[0] * P, hs[0] * P + width)

        def added(sub, i):
            s, hs = item(sub, i)
            return i + 1 if i < 2 * LEAD else HALF * (s + 1)

        def y_order(sub):
            last = ((2, 0), (3, 0), (2, 1), (3, 1)) if sub[0] == "mem" else ((2, 0), (2, 1), (3, 0), (3, 1))
            return ((0, 0), (0, 1), (1, 0), (1, 1)) + last

        def y_count(sub, g, h):
            return y_order(sub).index((g, h)) + 1

        SUBS = []
        for L in range(LAYERS):
            SUBS += [("mix", L), ("mem", L), ("ffn", L)]
        PRE = {"mix": 0, "mem": 2, "ffn": 3}
        POST = {"mix": g_mix_post, "mem": g_mem_post, "ffn": g_ffn_post}

        def prev_sub(sub):
            i = SUBS.index(sub)
            return SUBS[i - 1] if i else None

        def S(sub, name):
            return sem(f"{sub[0]}_{name}")

        def SV(sub, name, value):
            before = 0 if (name, sub[0]) == ("x_new", "mix") else PER_LAYER.get(name, 0)
            return sem(f"{sub[0]}_{name}"), value + sub[1] * before

        def gain(sub, kt):
            return gT[:, PRE[sub[0]], sub[1], kt:kt + 1]

        def pair_heads(q):
            return (2 * q, 2 * q + 1) if 0 <= q < HEADS // 2 else ()

        def m_out(h):
            return (tp if h < 2 else aux)[:, h % 2, 0:SEQ]

        block = ctx.enter_context(nc.Block())

        @block.sync
        def _(sp):
            def slab(n, s, src):
                if not (isinstance(n, int) and n < RING):
                    sp.wait_ge(lo_ready, n - (RING - 1))
                sp.dma_start(raw[:, s], src.rearrange("(j p) n -> p j n", p=P)).then_inc(raw_landed[s], 16)

            def groups(n0, w, cols, slabs):
                for g, c0 in enumerate(cols):
                    for s in range(slabs):
                        n = n0 + g * slabs + s
                        slab(n, n % RING, w[s * SLAB_KT * P:(s + 1) * SLAB_KT * P, c0:c0 + N])

            def groups_loop(n0, w, count, col0, stride, slabs, pair=1):
                with sp.Fori(0, count) as i:
                    for g in range(pair):
                        for s in range(slabs):
                            k = g * slabs + s
                            slab(i * (pair * slabs) + (n0 + k), k % RING,
                                 w[s * SLAB_KT * P:(s + 1) * SLAB_KT * P, bass.ds(i * stride + (col0 + g * N), N)])

            def load_gain(a, g):
                sp.dma_start(gain_in[a * LAYERS * KT:(a + 1) * LAYERS * KT, :],
                             g.rearrange("l (t p) -> (l t) p", p=P)).then_inc(small_landed, 16)

            sp.dma_start(ident[:], identity).then_inc(small_landed, 16)
            load_gain(0, g_mix_pre)
            w_ins, w_outs = (w_in_ab[0], w_in_c[0]), (w_out_ab[0], w_out_c[0])
            for L in range(LAYERS):
                n0 = L * LAYER_SLABS
                w_in, w_out = w_ins[L], w_outs[L]
                qkv = n0 + PHASE["qkv"]
                for s in range(GS):
                    if L == 0 and s < len(X_PIECES):
                        a, b = X_PIECES[s]
                        sp.dma_start(x_sb[:, :, a:b], x[0, :, a:b].rearrange("(h p) n -> p h n", p=P))\
                            .then_inc(x_landed[s], 16)
                    slab(qkv + s, (qkv + s) % RING, w_in[s * SLAB_KT * P:(s + 1) * SLAB_KT * P, 0:N])
                if L == 0:
                    for a, g in ((1, g_mem_kv), (2, g_mem_pre), (3, g_ffn_pre)):
                        load_gain(a, g)
                    with nc.allow_non_contiguous_dma(reason="positions, once"):
                        sp.dma_start(pos_i[:], positions[0].rearrange("(h p) -> p h", p=P)).then_inc(small_landed, 16)
                    sp.dma_start(invf[:], inv_freq).then_inc(small_landed, 16)
                if L:
                    sp.wait_ge(slab_used, n0)
                small = LS(L, "tables_landed")
                sp.dma_start(masks[:, 0, :], causal_mask).then_inc(small, 16)
                sp.dma_start(masks[:, 1, :], dilated_mask).then_inc(small, 16)
                for t in range(CW):
                    sp.dma_start(conv_in[:, t, :], conv_w[L, t].rearrange("(c p) -> c p", p=P)).then_inc(small, 16)
                sp.dma_start(conv_in[:, CW, :], conv_b[L].rearrange("(c p) -> c p", p=P)).then_inc(small, 16)
                groups(qkv + GS, w_in, [N], GS)
                pair = 2 * GS
                if L == 0:
                    groups(qkv + pair, w_in, [D // 2, D // 2 + N], GS)
                    groups_loop(qkv + 2 * pair, w_in, 2, 3 * D // 2, D // 2, GS, 2)
                    groups(qkv + 4 * pair, w_in, [D, D + N], GS)
                    groups(qkv + 5 * pair, w_in, [5 * D // 2, 5 * D // 2 + N], GS)
                else:
                    groups_loop(qkv + pair, w_in, 3, 2 * N, 2 * N, GS, 2)
                    groups(qkv + 4 * pair, w_in, [8 * N], GS)
                if L:
                    sp.wait_ge(*LV(L, "qk_t", 8))
                    sp.dma_start(wf_raw[:], w_in[:, 3 * D:3 * D + HEADS].rearrange("(t p) n -> p t n", p=P))\
                        .then_inc(small, 16)
                    sp.dma_start(bf_sb[:], b_f[0].rearrange("(h o) -> h o", o=1)).then_inc(small, 16)
                    groups(qkv + 4 * pair + GS, w_in, [9 * N, 10 * N, 11 * N], GS)
                groups(n0 + PHASE["mk"], w_mk[L], [0], GS)
                for g in range(D_GROUPS):
                    groups(n0 + PHASE["out"] + g * GS, w_out, [g * N], GS)
                groups(n0 + PHASE["mq"], w_mq[L], [0], GS)
                groups(n0 + PHASE["mv"], w_mv[L], [0], GS)
                for g in range(D_GROUPS):
                    groups(n0 + PHASE["mo"] + g * MEM_GS, w_mo[L], [g * N], MEM_GS)
                with sp.Fori(0, FF_GROUPS) as i:
                    for g in range(2):
                        for s in range(GS):
                            k = g * GS + s
                            slab(i * (2 * GS) + (n0 + PHASE["up"] + k), k % RING,
                                 w_up[L][s * SLAB_KT * P:(s + 1) * SLAB_KT * P, bass.ds(i * N + g * D_FF, N)])
                for g in range(D_GROUPS):
                    groups(n0 + PHASE["down"] + g * FF_GS, w_down[L], [g * N], FF_GS)
            for h in range(HALF):
                for c in range(D_GROUPS):
                    sp.wait_ge(sem("final_x"), D_GROUPS * h + c + 1)
                    sp.dma_start(out[0, h * P:(h + 1) * P, c * N:(c + 1) * N], x_sb[:, h, c * N:(c + 1) * N])\
                        .then_inc(out_stored, 16)
            sp.wait_ge(out_stored, 16 * HALF * D_GROUPS)

        @block.scalar
        def _(act):
            def split(n, s):
                act.wait_ge(raw_landed[s], landed(n, s))
                if not (isinstance(n, int) and n < RING):
                    act.wait_ge(slab_used, n - (RING - 1))
                act.activation(w_hi[:, s], raw[:, s], ACT.Copy).then_inc(hi_ready, 1)

            def landed(n, s):
                if isinstance(n, int):
                    return 16 * (n // RING + 1)
                return (n - s) * (16 // RING) + 16

            def ahead(n, s=None):
                if isinstance(n, int) and n + AHEAD >= TOTAL_SLABS:
                    return
                split(n + AHEAD, (n + AHEAD) % RING if s is None else (s + AHEAD) % RING)

            def norm_hi(sub, i):
                act.wait_ge(*SV(sub, "xT", i + 1))
                for j in range(SLAB_KT):
                    bank, kt, cols = item_tile(sub, i, j)
                    act.activation(a_hi[:, kt, cols], bank, ACT.Copy, scale=gain(sub, kt)).then_inc(S(sub, "a_hi"), 1)

            squared = {"last": None}

            def square(src, h, c, at, scratch, done):
                row, k = at
                if squared["last"]:
                    act.wait_ge(squared["last"], squared[squared["last"].name])
                act.activation(scratch[:], src, ACT.Square, scale=float(D) ** -0.5,
                               accum_out=stats[:, row, k + 2 * c + h:k + 2 * c + h + 1]).then_inc(done, 1)
                squared["last"] = done
                squared[done.name] = squared.get(done.name, 0) + 1

            def x_squares(sub, c):
                for h in range(HALF):
                    square(x_sb[:, h, c * N:(c + 1) * N], h, c, (0, 0), junk, S(sub, "x_sq"))

            def gain_chunk(sub, g):
                if g >= 2:
                    act.wait_ge(*SV(sub, "yg_done", y_count(sub, g - 2, 1)))
                elif prev_sub(sub):
                    act.wait_ge(*SV(prev_sub(sub), "yg_done", y_count(prev_sub(sub), 2 + g, 1)))
                row = POST[sub[0]][sub[1]:sub[1] + 1, g * N:(g + 1) * N]
                act.dma_start(g_post[:, g % 2, :], row.to_broadcast([P, N]))\
                    .then_inc(S(sub, f"g_landed_{g % 2}"), 16)

            def start(sub, n):
                split(n + 2, (n + 2) % RING)
                if sub == SUBS[0]:
                    norm_hi(sub, 4)
                    norm_hi(sub, 5)
                    split(n + 3, (n + 3) % RING)
                    norm_hi(sub, 6)
                else:
                    norm_hi(sub, 2)
                    split(n + 3, (n + 3) % RING)
                    for i in range(LEAD, 2 * LEAD + 1):
                        norm_hi(sub, i)
                for s in range(2, GS):
                    split(n + s + 2, (n + s + 2) % RING)
                    if 2 * LEAD + s - 1 < ITEMS:
                        norm_hi(sub, 2 * LEAD + s - 1)
                    if 2 <= s < 2 + D_GROUPS:
                        x_squares(sub, s - 2)
                    if s in (GS - 2, GS - 1):
                        gain_chunk(sub, s - (GS - 2))

            def y_square(sub, g, h, n_done):
                if n_done is None:
                    act.wait_ge(*SV(sub, "y_half", TAIL if g == D_GROUPS - 1 else TAIL - MEM_GS))
                else:
                    act.wait_ge(slab_used, n_done)
                over = sub[0] == "ffn" and (g, h) != (D_GROUPS - 1, 1)
                square(acc[:, g % 2, h, :], h, g, (3, 0), junk_ffn if over else junk, S(sub, "y_sq"))

            def tail(sub, after, e):
                ahead(e - 4)
                if sub[0] == "mem":
                    for h in range(HALF):
                        y_square(sub, 1, h, e - 2 * MEM_GS)
                ahead(e - 3)
                if sub[0] == "mem":
                    gain_chunk(sub, 3)
                    y_square(sub, 2, 0, None)
                y_square(sub, 3, 0, None)
                ahead(e - 2)
                if sub[0] == "mem":
                    y_square(sub, 2, 1, e - MEM_GS)
                if after:
                    norm_hi(after, 0)
                ahead(e - 1)
                if after:
                    norm_hi(after, 1)
                y_square(sub, 3, 1, e)

            for L in range(LAYERS):
                n0 = L * LAYER_SLABS
                mix, mm, ffn = ("mix", L), ("mem", L), ("ffn", L)
                if L == 0:
                    split(0, 0)
                    act.wait_ge(sem("gain_st"), 1)
                    norm_hi(mix, 0)
                    norm_hi(mix, 1)
                    split(1, 1)
                    norm_hi(mix, 2)
                    norm_hi(mix, 3)
                n = n0 + PHASE["qkv"]
                start(mix, n)

                def qk_evac(G, par):
                    act.wait_ge(slab_used, G * GS + (n0 + PHASE["qkv"] + GS))
                    act.wait_ge(*SV(mix, "rstd", 1))
                    if not (isinstance(G, int) and G < 2):
                        act.wait_ge(*LV(L, "qk_t", G - 1))
                    act.activation(qk_stage[:, par, 0, :], acc[:, par, 0, :], ACT.Copy,
                                   scale=stat(1, 0, 1)).then_inc(LS(L, "qk_ev_a"), 1)

                def qk_store(G):
                    act.wait_ge(*LV(L, "qk_t", G + 1))
                    act.activation(qkT[:, bass.ds(G * 4, 2), :],
                                   tp[:, 0, :].rearrange("p (a b) -> p a b", a=2), ACT.Copy)\
                        .then_inc(LS(L, "qk_st_a"), 1)

                def qk_group(G, par, n):
                    for s in range(GS):
                        if s == 0:
                            qk_evac(G - 1, 1 - par)
                        if s == 4:
                            qk_store(G - 1)
                        ahead(n + s, s)

                if L == 0:
                    act.wait_ge(sem("angles"), 1)
                    act.activation(sin_t[:], ang[:, 4], ACT.Sin).then_inc(sem("tables"), 1)
                    act.activation(cos_t[:], ang[:, 5], ACT.Sin, bias=half_pi[:], scale=-1.0).then_inc(sem("tables"), 1)
                qk_group(1, 1, n + GS)
                with act.Fori(1, 4) as i:
                    for k in range(2):
                        qk_group(i * 2 + k, k, i * (2 * GS) + (n + k * GS))

                def v_evac(vg):
                    act.wait_ge(slab_used, n0 + PHASE["qkv"] + (9 + vg) * GS)
                    act.activation(v_sb[:, 0, vg * N:(vg + 1) * N], acc[:, vg % 2, 0, :], ACT.Copy,
                                   scale=stat(1, 0, 1)).then_inc(LS(L, "v_ev_a"), 1)

                def load_mem(c):
                    act.dma_start(mem_in[:], mem[0, :, c * N:(c + 1) * N].rearrange("(h p) n -> p h n", p=P))\
                        .then_inc(LS(L, "mem_landed"), 16)

                def mem_step(q):
                    if q == -4:
                        load_mem(0)
                    if not 0 <= q < 4 * D_GROUPS:
                        return
                    c, r = q // 4, q % 4
                    if r in (1, 2):
                        m = 2 * c + r - 1
                        act.wait_ge(*LV(L, "mem_t", m + 1))
                        for j in range(SLAB_KT):
                            kt = SLAB_KT * m + j
                            act.activation(m_hi[:, kt, :], tp[:, m % 2, j * SEQ:(j + 1) * SEQ], ACT.Copy,
                                           scale=gT[:, 1, L, kt:kt + 1]).then_inc(LS(L, "m_hi"), 1)
                    if r == 2:
                        for h in range(HALF):
                            square(mem_in[:, h, :], h, c, (0, 8), junk, LS(L, "mem_sq"))
                        if c + 1 < D_GROUPS:
                            act.wait_ge(*LV(L, "mem_sq", HALF * (c + 1)))
                            load_mem(c + 1)

                for vg in range(4):
                    for s in range(GS):
                        if s == 0:
                            if vg == 0:
                                qk_evac(7, 1)
                            else:
                                v_evac(vg - 1)
                        if s == 4 and vg == 0:
                            qk_store(7)
                        if L and vg == 1 and s == 2:
                            act.wait_ge(*LV(L, "tables_landed", 16 * 8))
                            act.activation(wf_hi[:], wf_raw[:], ACT.Copy).then_inc(LS(L, "wf_hi"), 1)
                        if L and vg == 2 and s == 4:
                            act.wait_ge(*LV(L, "fg", 3))
                            act.activation(fabs[:], fabs[:], ACT.Exp, scale=-1.0).then_inc(LS(L, "fe"), 1)
                            act.wait_ge(*LV(L, "fe", 1))
                            act.activation(fabs[:], fabs[:], ACT.Ln, bias=1.0).then_inc(LS(L, "fe"), 1)
                        mem_step((vg - 1) * GS + s)
                        ahead(n + (8 + vg) * GS + s)

                def o_hi(h):
                    act.wait_ge(*LV(L, "o_t", h + 1))
                    act.activation(a_hi[:, h, :], acc[:, 1, h % 2, 0:SEQ], ACT.Copy).then_inc(LS(L, "o_hi"), 1)

                def probs(h):
                    act.wait_ge(*LV(L, "row_max", h + 1))
                    o = 8 * (h % 4)
                    for t, (a, b) in enumerate(((0, W0), (W0, W0 + W1))):
                        act.activation(prob[:, h % 4, a:b], prob[:, h % 4, a:b], ACT.Exp,
                                       bias=stats[:, 2, o + 2 + t:o + 3 + t],
                                       accum_out=stats[:, 2, o + 4 + t:o + 5 + t]).then_inc(LS(L, "exp"), 1)

                def prob_store(h):
                    act.wait_ge(*LV(L, "p_t", h + 1))
                    if h >= 2:
                        act.wait_ge(*LV(L, "o_t", h - 1))
                    act.activation(probT[:, h % 2, :], aux[:, h % 2, 0:W0 + W1], ACT.Copy).then_inc(LS(L, "p_st"), 1)

                def attend_first(q):
                    for h in pair_heads(q - 2):
                        o_hi(h)
                    for h in pair_heads(q):
                        probs(h)

                def attend_last(q):
                    for h in pair_heads(q - 1):
                        prob_store(h)

                def m_evac(n_done, par, dst, scale, done):
                    act.wait_ge(slab_used, n_done)
                    act.activation(dst[:, 0, :], acc[:, par, 0, :], ACT.Copy, scale=scale).then_inc(done, 1)

                n = n0 + PHASE["mk"]
                for s in range(GS):
                    if s == 0:
                        v_evac(3)
                    attend_first(s)
                    attend_last(s)
                    if s == GS - 1:
                        act.wait_ge(*LV(L, "m_rstd", 1))
                        m_evac(n + GS, 0, mk_stage, stat(1, 2, 3), LS(L, "m_ev_a"))
                    ahead(n + s)

                def y_group(sub, g, s, slabs, n):
                    if g and s == 0:
                        for h in range(HALF):
                            y_square(sub, g - 1, h, n + g * slabs)
                    if 1 <= g < D_GROUPS - 1 and s == 1:
                        gain_chunk(sub, g + 1)

                def m_store(k, dst):
                    act.wait_ge(*LV(L, "mqk_t", k + 1))
                    act.activation(dst[:, 0:2, :], aux[:, 0, :].rearrange("p (a b) -> p a b", a=2), ACT.Copy)\
                        .then_inc(LS(L, "mqk_st_a"), 1)

                n = n0 + PHASE["out"]
                for g in range(D_GROUPS):
                    for s in range(GS):
                        y_group(mix, g, s, GS, n)
                        if g * GS + s >= D_GROUPS * GS - TAIL:
                            continue
                        if g == 0:
                            if s == 0:
                                attend_last(GS)
                            attend_first(GS + s)
                            if s == 4:
                                m_store(0, mkT)
                        ahead(n + g * GS + s)
                n = n0 + PHASE["mq"]
                tail(mix, mm, n)
                start(mm, n)

                def m_probs(h):
                    act.wait_ge(*LV(L, "m_max", h + 1))
                    for t in range(HALF):
                        act.activation(mprob[:, h, t * SEQ:(t + 1) * SEQ], tp[:, h % 2, t * SEQ:(t + 1) * SEQ],
                                       ACT.Exp, scale=SCALE, bias=stats[:, 2, 8 * h + 2 + t:8 * h + 3 + t],
                                       accum_out=stats[:, 2, 8 * h + 4 + t:8 * h + 5 + t])\
                            .then_inc(LS(L, "m_exp"), 1)

                def m_prob_store(h):
                    act.wait_ge(*LV(L, "mp_t", h + 1))
                    act.activation(mprobT[:, h, :], aux[:, h % 2, :], ACT.Copy).then_inc(LS(L, "mp_st"), 1)

                n = n0 + PHASE["mv"]
                for s in range(GS):
                    if s == 0:
                        act.wait_ge(*SV(mm, "rstd", 1))
                        m_evac(n, 0, mq_stage, stat(1, 0, 1), LS(L, "m_ev_a"))
                    if s == 1:
                        m_store(1, mqT)
                    if s >= 4:
                        m_prob_store(s - 4)
                    if 2 <= s < 2 + MEM_HEADS:
                        m_probs(s - 2)
                    ahead(n + s)
                act.wait_ge(*LV(L, "mv_half", 1))
                act.activation(mv_sb[:, 0, :], acc[:, 1, 0, :], ACT.Copy, scale=stat(1, 2, 3)).then_inc(LS(L, "m_ev_a"), 1)
                for h in range(MEM_HEADS):
                    act.wait_ge(*LV(L, "mo_t", h + 1))
                    act.activation(a_hi[:, h, :], m_out(h), ACT.Copy).then_inc(LS(L, "mo_hi"), 1)
                n = n0 + PHASE["mo"]
                for g in range(2):
                    for s in range(MEM_GS):
                        y_group(mm, g, s, MEM_GS, n)
                        if g * MEM_GS + s < D_GROUPS * MEM_GS - TAIL:
                            ahead(n + g * MEM_GS + s)
                n = n0 + PHASE["up"]
                tail(mm, ffn, n)
                start(ffn, n)

                def u_evac(G, dst, par):
                    act.wait_ge(slab_used, G * GS + (n0 + PHASE["up"] + GS))
                    if not (isinstance(G, int) and G < 2):
                        act.wait_ge(*LV(L, "u_t", G - 1))
                    act.activation(dst[:, 0, :], acc[:, par, 0, :], ACT.Copy, scale=stat(1, 0, 1))\
                        .then_inc(LS(L, "u_ev_a"), 1)

                def conv_tap(G, src, dst, par, i):
                    act.wait_ge(*LV(L, "u_t", G + 1))
                    if not (isinstance(i, int) and i == 0):
                        act.wait_ge(*LV(L, "hid_lo", i))
                    for j in range(4):
                        c = i * 4 + (j + par * FF_KT)
                        act.activation(dst[:, j, :], src[:, j // 2, (j % 2) * SEQ:(j % 2 + 1) * SEQ], ACT.Identity,
                                       scale=tap(CW - 1, c), bias=tap(CW, c)).then_inc(LS(L, "tap_a"), 1)

                def tap(t, c):
                    return convT[:, t, bass.ds(c, 1)]

                def silu(i):
                    act.wait_ge(*LV(L, "conv_done", i * 16 + 8))
                    act.activation(conv_gate[:], conv_gate[:], ACT.Silu).then_inc(LS(L, "silu"), 1)

                def hid_hi_part(i):
                    act.wait_ge(*LV(L, "prod", i + 1))
                    act.activation(hid_hi[:, bass.ds(i * 4, 4), :], conv_val[:], ACT.Copy).then_inc(LS(L, "hid_hi"), 1)

                def val_tail(i, q):
                    if q == 0:
                        u_evac(i * 2 + 1, u_val, 1)
                    if q == 3:
                        conv_tap(i * 2 + 1, aux, conv_val, 1, i)
                    if q == 5:
                        hid_hi_part(i)

                def up_pair(i, n, first):
                    for q in range(GS if first else 0, 2 * GS):
                        if not first:
                            val_tail(i - 1, q)
                        if q == GS:
                            if first:
                                act.wait_ge(*SV(ffn, "rstd", 1))
                            u_evac(i * 2, u_gate, 0)
                        if q == GS + 3:
                            conv_tap(i * 2, tp, conv_gate, 0, i)
                        if q == GS + 4:
                            silu(i)
                        ahead(n + q, q)

                up_pair(0, n, True)
                with act.Fori(1, FF_GROUPS) as i:
                    up_pair(i, i * (2 * GS) + n, False)
                n = n0 + PHASE["down"]
                for g in range(D_GROUPS):
                    for s in range(FF_GS):
                        if g == 0:
                            val_tail(FF_GROUPS - 1, s)
                        y_group(ffn, g, s, FF_GS, n)
                        if g * FF_GS + s < D_GROUPS * FF_GS - TAIL:
                            ahead(n + g * FF_GS + s)
                tail(ffn, ("mix", L + 1) if L + 1 < LAYERS else None, n + D_GROUPS * FF_GS)

        @block.vector
        def _(dve):
            def split(n, s):
                dve.wait_ge(hi_ready, n + 1)
                dve.tensor_tensor(w_lo[:, s], raw[:, s], w_hi[:, s].bitcast(F32), ALU.subtract).then_inc(lo_ready, 1)

            def ahead(n, s=None):
                if isinstance(n, int) and n + AHEAD >= TOTAL_SLABS:
                    return
                split(n + AHEAD, (n + AHEAD) % RING if s is None else (s + AHEAD) % RING)

            def add_y(before, h, x0, width, done):
                dve.wait_ge(*SV(before, "y_rstd", h + 1))
                dve.wait_ge(*SV(before, "yg_done", y_count(before, 3, h)))
                xs = x_sb[:, h, x0:x0 + width]
                dve.scalar_tensor_tensor(out=xs, in0=yg[:, h, x0:x0 + width], scalar=stat(1, 4 + h, 5 + h),
                                         in1=xs, op0=ALU.mult, op1=ALU.add).then_inc(done, 1)

            def norm_add(sub, i):
                s, hs = item(sub, i)
                if prev_sub(sub):
                    for h in hs:
                        add_y(prev_sub(sub), h, s * SLAB_KT * P, SLAB_KT * P, S(sub, "x_new"))

            def norm_lo(sub, i):
                dve.wait_ge(*SV(sub, "a_hi", SLAB_KT * (i + 1)))
                for j in range(SLAB_KT):
                    bank, kt, cols = item_tile(sub, i, j)
                    dve.scalar_tensor_tensor(out=a_lo[:, kt, cols], in0=bank, scalar=gain(sub, kt),
                                             in1=a_hi[:, kt, cols].bitcast(F32),
                                             op0=ALU.mult, op1=ALU.subtract).then_inc(S(sub, "a_lo"), 1)

            def y_gain(sub, g, h):
                dve.wait_ge(*SV(sub, f"g_landed_{g % 2}", 16 * (g // 2 + 1)))
                dve.wait_ge(*SV(sub, "y_sq", y_count(sub, g, h)))
                dve.tensor_tensor(yg[:, h, g * N:(g + 1) * N], acc[:, g % 2, h, :], g_post[:, g % 2, :], ALU.mult)\
                    .then_inc(S(sub, "yg_done"), 1)

            def angles():
                two_pi = 2 * np.pi
                c1 = 6.28125
                c2 = float(np.float32(np.floor((two_pi - c1) * 2 ** 17) / 2 ** 17))
                c3 = float(np.float32(np.floor((two_pi - c1 - c2) * 2 ** 26) / 2 ** 26))
                c4 = float(np.float32(two_pi - c1 - c2 - c3))
                magic = 1.5 * 2.0 ** 23
                step = [0]
                chain = sem("angle_steps")

                def then(i):
                    step[0] += 1
                    i.then_inc(chain, 1)
                    dve.wait_ge(chain, step[0])

                dve.wait_ge(small_landed, 16 * 7)
                then(dve.tensor_copy(pos_f[:], pos_i[:]))
                for h in range(HALF):
                    then(dve.tensor_scalar(ang[:, 0, h, :], invf[:], pos_f[:, h:h + 1], None, ALU.mult))
                then(dve.tensor_scalar(ang[:, 1], ang[:, 0], 1.0 / two_pi, None, ALU.mult))
                then(dve.tensor_scalar(ang[:, 2], ang[:, 1], magic, None, ALU.add))
                then(dve.tensor_scalar(ang[:, 1], ang[:, 2], -magic, None, ALU.add))
                for k, (c, a, b) in enumerate(((c1, 0, 2), (c2, 2, 3), (c3, 3, 2), (c4, 2, 3))):
                    then(dve.scalar_tensor_tensor(out=ang[:, b], in0=ang[:, 1], scalar=-c, in1=ang[:, a],
                                                  op0=ALU.mult, op1=ALU.add))
                edge = float(np.nextafter(np.float32(np.pi), np.float32(0)))
                then(dve.tensor_scalar(ang[:, 4], ang[:, 3], edge, -edge, ALU.min, ALU.max))
                then(dve.tensor_scalar(ang[:, 2], ang[:, 4], -1.0, None, ALU.mult))
                dve.tensor_tensor(ang[:, 5], ang[:, 2], ang[:, 4], ALU.max).then_inc(sem("angles"), 1)

            def start(sub, n):
                if sub == SUBS[0]:
                    split(n + 2, (n + 2) % RING)
                    norm_lo(sub, 4)
                    norm_lo(sub, 5)
                    split(n + 3, (n + 3) % RING)
                    norm_lo(sub, 6)
                else:
                    norm_add(sub, 3)
                    split(n + 2, (n + 2) % RING)
                    norm_lo(sub, 2)
                    norm_lo(sub, 3)
                    norm_add(sub, 4)
                    norm_add(sub, 5)
                    norm_lo(sub, 4)
                    norm_add(sub, 6)
                    norm_lo(sub, 5)
                    split(n + 3, (n + 3) % RING)
                    norm_add(sub, 7)
                    norm_lo(sub, 6)
                for s in range(2, GS):
                    if sub == SUBS[0] and s == GS - 4:
                        angles()
                    if 2 * LEAD + s < ITEMS:
                        norm_add(sub, 2 * LEAD + s)
                    split(n + s + 2, (n + s + 2) % RING)
                    if 2 * LEAD + s - 1 < ITEMS:
                        norm_lo(sub, 2 * LEAD + s - 1)

            def tail(sub, after, e):
                ahead(e - 4)
                if sub[0] == "mem":
                    for h in range(HALF):
                        y_gain(sub, 1, h)
                ahead(e - 3)
                if sub[0] == "mem":
                    y_gain(sub, 2, 0)
                y_gain(sub, 3, 0)
                for i in range(LEAD):
                    norm_add(after, i)
                ahead(e - 2)
                if sub[0] == "mem":
                    y_gain(sub, 2, 1)
                norm_lo(after, 0)
                ahead(e - 1)
                norm_lo(after, 1)
                y_gain(sub, 3, 1)

            dve.memset(minus_half[:], -0.5).then_inc(sem("consts"), 1)
            dve.memset(half_pi[:], float(np.pi / 2)).then_inc(sem("consts"), 1)
            dve.wait_ge(sem("gain_t"), 1)
            dve.tensor_copy(gT[:, 0].rearrange("p l k -> p (l k)"), aux[:, 0, 0:LAYERS * KT]).then_inc(sem("gain_st"), 1)
            for L in range(LAYERS):
                n0 = L * LAYER_SLABS
                mix, mm, ffn = ("mix", L), ("mem", L), ("ffn", L)
                n = n0 + PHASE["qkv"]
                if L == 0:
                    split(0, 0)
                    dve.wait_ge(sem("gain_st"), 1)
                    norm_lo(mix, 0)
                    norm_lo(mix, 1)
                    split(1, 1)
                    norm_lo(mix, 2)
                    norm_lo(mix, 3)
                start(mix, n)

                def qk_evac(G, par):
                    dve.wait_ge(slab_used, G * GS + (n0 + PHASE["qkv"] + GS))
                    dve.wait_ge(*SV(mix, "rstd", 1))
                    if not (isinstance(G, int) and G < 2):
                        dve.wait_ge(*LV(L, "qk_t", G - 1))
                    dve.tensor_scalar(qk_stage[:, par, 1, :], acc[:, par, 1, :], stat(1, 1, 2), None, ALU.mult)\
                        .then_inc(LS(L, "qk_ev_d"), 1)
                    if L == 0:
                        if isinstance(G, int) and G == 0:
                            dve.wait_ge(sem("tables"), 2)
                        dve.wait_ge(*LV(L, "qk_ev_a", G + 1))
                        dve.wait_ge(*LV(L, "qk_ev_d", G + 1))
                        heads = qk_stage[:, par].rearrange("p h (a e) -> p h a e", e=P)
                        r1, r2 = heads[:, :, :, 0:ROT_HALF], heads[:, :, :, ROT_HALF:ROT]
                        for h in range(HALF):
                            c = cos_t[:, h:h + 1, :].to_broadcast([P, 4, ROT_HALF])
                            sn = sin_t[:, h:h + 1, :].to_broadcast([P, 4, ROT_HALF])
                            for k, (r, f) in enumerate(((r1, c), (r2, sn), (r2, c), (r1, sn))):
                                dve.tensor_tensor(rope_t[:, k, h], r[:, h], f, ALU.mult).then_inc(LS(L, "rope"), 1)
                        dve.wait_ge(*LV(L, "rope", G * 10 + 8))
                        dve.tensor_tensor(r1, rope_t[:, 0], rope_t[:, 1], ALU.subtract).then_inc(LS(L, "rope"), 1)
                        dve.tensor_tensor(r2, rope_t[:, 2], rope_t[:, 3], ALU.add).then_inc(LS(L, "rope"), 1)

                def qk_store(G):
                    dve.wait_ge(*LV(L, "qk_t", G + 1))
                    dve.tensor_copy(qkT[:, bass.ds(G * 4 + 2, 2), :], tp[:, 1, :].rearrange("p (a b) -> p a b", a=2))\
                        .then_inc(LS(L, "qk_st_d"), 1)

                def qk_group(G, par, n):
                    for s in range(GS):
                        if s == 0:
                            qk_evac(G - 1, 1 - par)
                        if s == 4:
                            qk_store(G - 1)
                        ahead(n + s, s)

                if L == 0:
                    dve.wait_ge(sem("gain_t"), 2)
                    dve.tensor_copy(gT[:, 1:].rearrange("p a l k -> p (a l k)"), aux[:, 0, LAYERS * KT:P])\
                        .then_inc(sem("gain_st"), 1)
                qk_group(1, 1, n + GS)
                with dve.Fori(1, 4) as i:
                    for k in range(2):
                        qk_group(i * 2 + k, k, i * (2 * GS) + (n + k * GS))

                def v_evac(vg):
                    dve.wait_ge(slab_used, n0 + PHASE["qkv"] + (9 + vg) * GS)
                    dve.tensor_scalar(v_sb[:, 1, vg * N:(vg + 1) * N], acc[:, vg % 2, 1, :], stat(1, 1, 2), None,
                                      ALU.mult).then_inc(LS(L, "v_ev_d"), 1)

                def mem_step(q):
                    if 0 <= q < 4 * D_GROUPS and q % 4 in (1, 2):
                        m = 2 * (q // 4) + q % 4 - 1
                        dve.wait_ge(*LV(L, "m_hi", SLAB_KT * (m + 1)))
                        for j in range(SLAB_KT):
                            kt = SLAB_KT * m + j
                            dve.scalar_tensor_tensor(out=m_lo[:, kt, :], in0=tp[:, m % 2, j * SEQ:(j + 1) * SEQ],
                                                     scalar=gT[:, 1, L, kt:kt + 1], in1=m_hi[:, kt, :].bitcast(F32),
                                                     op0=ALU.mult, op1=ALU.subtract).then_inc(LS(L, "m_lo"), 1)

                for vg in range(4):
                    for s in range(GS):
                        if s == 0:
                            if vg == 0:
                                qk_evac(7, 1)
                            else:
                                v_evac(vg - 1)
                        if s == 4 and vg == 0:
                            qk_store(7)
                        if L and vg == 1 and s == 2:
                            dve.wait_ge(*LV(L, "wf_hi", 1))
                            dve.tensor_tensor(wf_lo[:], wf_raw[:], wf_hi[:].bitcast(F32), ALU.subtract)\
                                .then_inc(LS(L, "wf_lo"), 1)
                        if L and vg == 1 and s == 6:
                            fg = LS(L, "fg")
                            dve.wait_ge(*LV(L, "fg_mm", 1))
                            dve.tensor_copy(fabs[:], aux[0:HEADS, 1, 0:SEQ]).then_inc(LS(L, "fg_st"), 1)
                            dve.wait_ge(*LV(L, "fg_st", 1))
                            dve.tensor_tensor(fones[:], aux[0:HEADS, 0, 0:SEQ], fabs[:], ALU.mult).then_inc(LS(L, "fg_st"), 1)
                            dve.wait_ge(*LV(L, "fg_st", 2))
                            dve.tensor_scalar(fz[:], fones[:], bf_sb[:], None, ALU.add).then_inc(fg, 1)
                            dve.tensor_scalar(fneg[:], fones[:], bf_sb[:], 0.0, ALU.add, ALU.min).then_inc(fg, 1)
                            dve.wait_ge(fg, 2)
                            dve.scalar_tensor_tensor(out=fabs[:], in0=fneg[:], scalar=-2.0, in1=fz[:],
                                                     op0=ALU.mult, op1=ALU.add).then_inc(fg, 1)
                            dve.memset(fones[:], 1.0).then_inc(LS(L, "fg_st"), 1)
                            dve.memset(fb[:].bitcast(F32), 0.0).then_inc(LS(L, "fg_st"), 1)
                            dve.tensor_tensor(sel[:], ident[0:P // 2, 0:HEADS], ident[0:P // 2, 32:32 + HEADS], ALU.add)\
                                .then_inc(LS(L, "fg_st"), 1)
                        if L and vg == 3 and s == 1:
                            fg = LS(L, "fg")
                            dve.wait_ge(*LV(L, "fe", 2))
                            dve.tensor_tensor(fz[:], fabs[:], fneg[:], ALU.subtract).then_inc(fg, 1)
                            dve.wait_ge(fg, 4)
                            dve.wait_ge(*LV(L, "fg_st", 5))
                            dve.tensor_tensor_scan(fneg[:], fones[:], fz[:], 0.0, ALU.mult, ALU.add).then_inc(fg, 1)
                            dve.wait_ge(fg, 5)
                            dve.tensor_scalar(fbias[:], fneg[:], 1.0 / SCALE, None, ALU.mult).then_inc(fg, 1)
                            dve.wait_ge(fg, 6)
                            dve.tensor_copy(fb[0:HEADS, :], fbias[:]).then_inc(fg, 1)
                            dve.wait_ge(fg, 7)
                            dve.tensor_tensor(fb[32:32 + HEADS, :], fbias[:], fb[0:HEADS, :].bitcast(F32), ALU.subtract)\
                                .then_inc(LS(L, "fbias"), 1)
                        mem_step((vg - 1) * GS + s)
                        ahead(n + (8 + vg) * GS + s)

                def scores(h):
                    mask = 1 if (L == 0 and h < HEADS // 2) else 0
                    if h == 0:
                        dve.wait_ge(*LV(L, "tables_landed", 16 * (8 if L else 6)))
                    if h >= 4:
                        dve.wait_ge(*LV(L, "p_t", h - 3))
                    dve.wait_ge(*LV(L, "s", h + 1))
                    o = 8 * (h % 4)
                    for t, (a, b) in enumerate(((0, W0), (W0, W0 + W1))):
                        dve.tensor_tensor_reduce(prob[:, h % 4, a:b], tp[:, h % 2, a:b], masks[:, mask, a:b],
                                                 SCALE, 3.0 * MASKED, ALU.add, ALU.max,
                                                 stats[:, 2, o + t:o + t + 1]).then_inc(LS(L, "s_max"), 1)
                    dve.wait_ge(*LV(L, "s_max", 2 * (h + 1)))
                    dve.tensor_scalar(stats[:, 2, o + 2:o + 4], stats[:, 2, o:o + 2], -1.0, None, ALU.mult)\
                        .then_inc(LS(L, "row_max"), 1)

                def normalise(h):
                    o = 8 * (h % 4)
                    dve.wait_ge(*LV(L, "exp", 2 * (h + 1)))
                    dve.reciprocal(stats[:, 2, o + 6:o + 8], stats[:, 2, o + 4:o + 6]).then_inc(LS(L, "recip"), 1)
                    dve.wait_ge(*LV(L, "recip", h + 1))
                    for t, (a, b) in enumerate(((0, W0), (W0, W0 + W1))):
                        dve.tensor_scalar(prob[:, h % 4, a:b], prob[:, h % 4, a:b],
                                          stats[:, 2, o + 6 + t:o + 7 + t], None, ALU.mult)\
                            .then_inc(LS(L, "p"), 1)

                def o_lo(h):
                    dve.wait_ge(*LV(L, "o_hi", h + 1))
                    dve.tensor_tensor(a_lo[:, h, :], acc[:, 1, h % 2, 0:SEQ], a_hi[:, h, :].bitcast(F32),
                                      ALU.subtract).then_inc(LS(L, "o_lo"), 1)

                def attend_first(q):
                    for h in pair_heads(q):
                        scores(h)
                    for h in pair_heads(q - 2):
                        o_lo(h)

                def attend_last(q):
                    for h in pair_heads(q):
                        normalise(h)

                def m_evac(n_done, par, dst, scale, done):
                    dve.wait_ge(slab_used, n_done)
                    dve.tensor_scalar(dst[:, 1, :], acc[:, par, 1, :], scale, None, ALU.mult).then_inc(done, 1)

                n = n0 + PHASE["mk"]
                for s in range(GS):
                    if s == 0:
                        v_evac(3)
                    attend_first(s)
                    attend_last(s)
                    if s == GS - 1:
                        dve.wait_ge(*LV(L, "m_rstd", 1))
                        m_evac(n + GS, 0, mk_stage, stat(1, 3, 4), LS(L, "m_ev_d"))
                    ahead(n + s)

                def m_store(k, dst):
                    dve.wait_ge(*LV(L, "mqk_t", k + 1))
                    dve.tensor_copy(dst[:, 2:4, :], aux[:, 1, :].rearrange("p (a b) -> p a b", a=2))\
                        .then_inc(LS(L, "mqk_st_d"), 1)

                n = n0 + PHASE["out"]
                for g in range(D_GROUPS):
                    for s in range(GS):
                        if g and s == 0:
                            for h in range(HALF):
                                y_gain(mix, g - 1, h)
                        if g * GS + s >= D_GROUPS * GS - TAIL:
                            continue
                        if g == 0:
                            attend_first(GS + s)
                            if s == 4:
                                m_store(0, mkT)
                            if s == 6:
                                dve.wait_ge(*LV(L, "conv_t", 1))
                                dve.tensor_copy(convT[:], tp[:, 0, 0:(CW + 1) * FF_TILES]
                                                .rearrange("p (t c) -> p t c", t=CW + 1)).then_inc(LS(L, "conv_st"), 1)
                        ahead(n + g * GS + s)
                n = n0 + PHASE["mq"]
                tail(mix, mm, n)
                start(mm, n)

                def m_scores(h):
                    dve.wait_ge(*LV(L, "ms", h + 1))
                    o = 8 * h
                    dve.tensor_reduce(stats[:, 2, o:o + 2], tp[:, h % 2, :].rearrange("p (t k) -> p t k", t=HALF),
                                      AX.X, ALU.max).then_inc(LS(L, "ms_max"), 1)
                    dve.wait_ge(*LV(L, "ms_max", h + 1))
                    dve.tensor_scalar(stats[:, 2, o + 2:o + 4], stats[:, 2, o:o + 2], -SCALE, None, ALU.mult)\
                        .then_inc(LS(L, "m_max"), 1)

                def m_normalise(h):
                    o = 8 * h
                    dve.wait_ge(*LV(L, "m_exp", 2 * (h + 1)))
                    dve.reciprocal(stats[:, 2, o + 6:o + 8], stats[:, 2, o + 4:o + 6]).then_inc(LS(L, "m_recip"), 1)
                    dve.wait_ge(*LV(L, "m_recip", h + 1))
                    for t in range(HALF):
                        pr = mprob[:, h, t * SEQ:(t + 1) * SEQ]
                        dve.tensor_scalar(pr, pr, stats[:, 2, o + 6 + t:o + 7 + t], None, ALU.mult)\
                            .then_inc(LS(L, "mp"), 1)

                n = n0 + PHASE["mv"]
                for s in range(GS):
                    if s == 0:
                        dve.wait_ge(*SV(mm, "rstd", 1))
                        m_evac(n, 0, mq_stage, stat(1, 1, 2), LS(L, "m_ev_d"))
                    if s == 1:
                        m_store(1, mqT)
                    if 2 <= s < 2 + MEM_HEADS:
                        m_scores(s - 2)
                    if 3 <= s < 3 + MEM_HEADS:
                        m_normalise(s - 3)
                    ahead(n + s)
                m_evac(n + GS, 1, mv_sb, stat(1, 3, 4), LS(L, "m_ev_d"))
                for h in range(MEM_HEADS):
                    dve.wait_ge(*LV(L, "mo_hi", h + 1))
                    dve.tensor_tensor(a_lo[:, h, :], m_out(h), a_hi[:, h, :].bitcast(F32), ALU.subtract)\
                        .then_inc(LS(L, "mo_lo"), 1)
                n = n0 + PHASE["mo"]
                for g in range(2):
                    for s in range(MEM_GS):
                        if g and s == 0:
                            for h in range(HALF):
                                y_gain(mm, g - 1, h)
                        ahead(n + g * MEM_GS + s)
                n = n0 + PHASE["up"]
                tail(mm, ffn, n)
                start(ffn, n)

                def u_evac(G, dst, par):
                    dve.wait_ge(slab_used, G * GS + (n0 + PHASE["up"] + GS))
                    if not (isinstance(G, int) and G < 2):
                        dve.wait_ge(*LV(L, "u_t", G - 1))
                    dve.tensor_scalar(dst[:, 1, :], acc[:, par, 1, :], stat(1, 1, 2), None, ALU.mult)\
                        .then_inc(LS(L, "u_ev_d"), 1)

                def conv_taps(G, src, dst, par, i):
                    for j in range(4):
                        c = i * 4 + (j + par * FF_KT)
                        dve.wait_ge(*LV(L, "tap_a", G * 4 + 2 * (j // 2 + 1)))
                        u = src[:, j // 2, (j % 2) * SEQ:(j % 2 + 1) * SEQ]
                        o = dst[:, j, :]
                        dve.scalar_tensor_tensor(out=o[:, 1:SEQ], in0=u[:, 0:SEQ - 1], scalar=convT[:, 1, bass.ds(c, 1)],
                                                 in1=o[:, 1:SEQ], op0=ALU.mult, op1=ALU.add)\
                            .then_inc(LS(L, "conv_done"), 1)
                    for j in range(4):
                        c = i * 4 + (j + par * FF_KT)
                        u = src[:, j // 2, (j % 2) * SEQ:(j % 2 + 1) * SEQ]
                        o = dst[:, j, :]
                        dve.wait_ge(*LV(L, "conv_done", G * 8 + (j + 1)))
                        dve.scalar_tensor_tensor(out=o[:, 2:SEQ], in0=u[:, 0:SEQ - 2], scalar=convT[:, 0, bass.ds(c, 1)],
                                                 in1=o[:, 2:SEQ], op0=ALU.mult, op1=ALU.add)\
                            .then_inc(LS(L, "conv_done"), 1)

                def val_tail(i, q):
                    if q == 0:
                        u_evac(i * 2 + 1, u_val, 1)
                    if q == 3:
                        conv_taps(i * 2 + 1, aux, conv_val, 1, i)
                    if q == 4:
                        dve.wait_ge(*LV(L, "silu", i + 1))
                        dve.wait_ge(*LV(L, "conv_done", i * 16 + 16))
                        dve.tensor_tensor(conv_val[:], conv_gate[:], conv_val[:], ALU.mult).then_inc(LS(L, "prod"), 1)
                    if q == 5:
                        dve.wait_ge(*LV(L, "hid_hi", i + 1))
                        dve.tensor_tensor(hid_lo[:, bass.ds(i * 4, 4), :], conv_val[:],
                                          hid_hi[:, bass.ds(i * 4, 4), :].bitcast(F32), ALU.subtract)\
                            .then_inc(LS(L, "hid_lo"), 1)

                def up_pair(i, n, first):
                    for q in range(GS if first else 0, 2 * GS):
                        if not first:
                            val_tail(i - 1, q)
                        if q == GS:
                            if first:
                                dve.wait_ge(*SV(ffn, "rstd", 1))
                            u_evac(i * 2, u_gate, 0)
                        if q == GS + 3:
                            conv_taps(i * 2, tp, conv_gate, 0, i)
                        ahead(n + q, q)

                up_pair(0, n, True)
                with dve.Fori(1, FF_GROUPS) as i:
                    up_pair(i, i * (2 * GS) + n, False)
                n = n0 + PHASE["down"]
                for g in range(D_GROUPS):
                    for s in range(FF_GS):
                        if g == 0:
                            val_tail(FF_GROUPS - 1, s)
                        if g and s == 0:
                            for h in range(HALF):
                                y_gain(ffn, g - 1, h)
                        if g * FF_GS + s < D_GROUPS * FF_GS - TAIL:
                            ahead(n + g * FF_GS + s)
                if L + 1 < LAYERS:
                    tail(ffn, ("mix", L + 1), n + D_GROUPS * FF_GS)
            e = TOTAL_SLABS
            ahead(e - 4)
            ahead(e - 3)
            for h in range(HALF):
                y_gain(SUBS[-1], 3, h)
                for c in range(D_GROUPS):
                    add_y(SUBS[-1], h, c * N, N, sem("final_x"))

        @block.gpsimd
        def _(pool):
            def two(at):
                row, k = at
                return lambda h=None: stats[:, row, k:k + 2] if h is None else stats[:, row, k + h:k + h + 1]

            def rstd(layer, row, at, to, chain, done):
                g = [two((row, at + 2 * c)) for c in range(D_GROUPS)]
                t = [two((1, 16 + 2 * k)) for k in range(3)]
                pool.tensor_tensor(t[0](), g[0](), g[1](), ALU.add).then_inc(chain, 1)
                pool.wait_ge(chain, 4 * layer + 1)
                pool.tensor_tensor(t[1](), t[0](), g[2](), ALU.add).then_inc(chain, 1)
                pool.wait_ge(chain, 4 * layer + 2)
                pool.tensor_tensor(t[0](), t[1](), g[3](), ALU.add).then_inc(chain, 1)
                pool.wait_ge(chain, 4 * layer + 3)
                pool.tensor_scalar(t[2](), t[0](), EPS, None, ALU.add).then_inc(chain, 1)
                pool.wait_ge(chain, 4 * layer + 4)
                pool.tensor_tensor(two((1, to))(), t[2](), minus_half[:], ALU.pow).then_inc(done, 1)

            def y_rstd(sub):
                g = [two((3, 2 * c)) for c in range(D_GROUPS)]
                t = [two((1, 22 + 2 * k)) for k in range(4)]
                chain, c0 = SV(sub, "yc", 0)
                pool.wait_ge(*SV(sub, "y_sq", y_count(sub, 1, 1)))
                pool.tensor_tensor(t[0](), g[0](), g[1](), ALU.add).then_inc(chain, 1)
                pool.wait_ge(chain, c0 + 1)
                pool.tensor_scalar(t[1](), t[0](), EPS, None, ALU.add).then_inc(chain, 1)
                pool.wait_ge(chain, c0 + 2)
                for h in range(HALF):
                    pool.wait_ge(*SV(sub, "y_sq", y_count(sub, 2, h)))
                    pool.tensor_tensor(t[2](h), t[1](h), g[2](h), ALU.add).then_inc(chain, 1)
                    pool.wait_ge(chain, c0 + 3 + 2 * h)
                    pool.wait_ge(*SV(sub, "y_sq", y_count(sub, 3, h)))
                    pool.tensor_tensor(t[3](h), t[2](h), g[3](h), ALU.add).then_inc(chain, 1)
                    pool.wait_ge(chain, c0 + 4 + 2 * h)
                    pool.tensor_tensor(two((1, 4))(h), t[3](h), minus_half[:, 0:1], ALU.pow)\
                        .then_inc(S(sub, "y_rstd"), 1)

            def x_rstd(sub):
                pool.wait_ge(*SV(sub, "x_sq", HALF * 4))
                rstd(sub[1], 0, 0, 0, S(sub, "xc"), S(sub, "rstd"))

            pool.wait_ge(sem("consts"), 2)
            for L in range(LAYERS):
                x_rstd(("mix", L))
                pool.wait_ge(*LV(L, "mem_sq", HALF * 4))
                rstd(L, 0, 8, 2, LS(L, "mc"), LS(L, "m_rstd"))
                y_rstd(("mix", L))
                x_rstd(("mem", L))
                y_rstd(("mem", L))
                x_rstd(("ffn", L))
                y_rstd(("ffn", L))

        @block.tensor
        def _(pe):
            def half_slab(h, slot, par, k0, kts, hi, lo, ready=None):
                rows = slice(h * P, (h + 1) * P)
                o = acc[:, par, h, :]
                for j in range(SLAB_KT):
                    kt = k0 + j
                    if ready:
                        pe.wait_ge(ready[0], ready[1] + j)
                    pe.matmul(o, hi[:, kt, rows], w_hi[:, slot, j, :], start=(kt == 0), stop=False)
                    pe.matmul(o, hi[:, kt, rows], w_lo[:, slot, j, :], start=False, stop=False)
                    last = pe.matmul(o, lo[:, kt, rows], w_hi[:, slot, j, :], start=False, stop=(kt == kts - 1))
                return last

            def slab(n, slot, par, k0, kts, hi, lo, ready=None):
                pe.wait_ge(lo_ready, n + 1)
                for h in range(HALF):
                    last = half_slab(h, slot, par, k0, kts, hi, lo, ready if h == 0 else None)
                last.then_inc(slab_used, 1)

            def transposes(dst, src, tiles, done):
                for j in range(tiles):
                    for h in range(HALF):
                        last = pe.transpose(dst(j, h), src(j, h), ident[:])
                if done is not None:
                    last.then_inc(done, 1)
                return last

            def norm_turn(sub, i):
                s, hs = item(sub, i)
                if prev_sub(sub):
                    pe.wait_ge(*SV(sub, "x_new", added(sub, i)))
                elif i == 0 or item(sub, i - 1)[0] != s:
                    pe.wait_ge(x_landed[[a <= s * SLAB_KT * P < b for a, b in X_PIECES].index(True)], 16)
                if i >= 4:
                    pe.wait_ge(*SV(sub, "a_lo", SLAB_KT * (i - 3)))
                for j in range(SLAB_KT):
                    to, kt, _ = item_tile(sub, i, j)
                    for k, h in enumerate(hs):
                        last = pe.transpose(to[:, k * P:(k + 1) * P], x_sb[:, h, kt * P:(kt + 1) * P], ident[:])
                last.then_inc(S(sub, "xT"), 1)

            def a_ready(sub, i):
                return SV(sub, "a_lo", SLAB_KT * i + 1)

            def start(sub, n):
                for s in range(LEAD if sub == SUBS[0] else 0):
                    pe.wait_ge(lo_ready, n + s + 1)
                    for h in range(HALF):
                        last = half_slab(h, (n + s) % RING, 0, SLAB_KT * s, KT, a_hi, a_lo, a_ready(sub, 2 * s + h))
                    last.then_inc(slab_used, 1)
                    for i in ((4, 5), (6,), (7,))[s]:
                        norm_turn(sub, i)
                for s in range(LEAD if sub != SUBS[0] else 0):
                    pe.wait_ge(lo_ready, n + s + 1)
                    half_slab(0, (n + s) % RING, 0, SLAB_KT * s, KT, a_hi, a_lo, a_ready(sub, s))
                    if s >= 1:
                        norm_turn(sub, LEAD + s - 1)
                for s in range(LEAD if sub != SUBS[0] else 0):
                    half_slab(1, (n + s) % RING, 0, SLAB_KT * s, KT, a_hi, a_lo, a_ready(sub, LEAD + s))\
                        .then_inc(slab_used, 1)
                    norm_turn(sub, 2 * LEAD - 1 + s)
                for s in range(LEAD, GS):
                    slab(n + s, (n + s) % RING, 0, SLAB_KT * s, KT, a_hi, a_lo, a_ready(sub, LEAD + s))
                    if LEAD + s + 2 < ITEMS:
                        norm_turn(sub, LEAD + s + 2)

            def tail(sub, after, e, kts, hi, lo):
                per = kts // SLAB_KT
                for h in range(HALF):
                    for k in range(TAIL):
                        at = D_GROUPS * per - TAIL + k
                        g, s = at // per, at % per
                        if h == 0:
                            if s == 0:
                                y_free(sub, g)
                            pe.wait_ge(lo_ready, e - TAIL + k + 1)
                        last = half_slab(h, (e - TAIL + k) % RING, g % 2, SLAB_KT * s, kts, hi, lo)
                        last.then_inc(slab_used if h else S(sub, "y_half"), 1)
                        if h and k and after:
                            norm_turn(after, k - 1)

            def y_free(sub, g):
                if g >= 2:
                    done = HALF * D_GROUPS if g > D_GROUPS else y_count(sub, g - 2, 1)
                    pe.wait_ge(*SV(sub, "y_sq", done))
                    pe.wait_ge(*SV(sub, "yg_done", done))

            g0 = LAYERS * KT
            pe.wait_ge(small_landed, 16 * 2)
            pe.transpose(aux[:, 0, 0:g0], gain_in[0:g0, :], ident[0:g0, 0:g0]).then_inc(sem("gain_t"), 1)
            pe.wait_ge(sem("gain_st"), 1)
            for i in range(4):
                norm_turn(SUBS[0], i)
            for L in range(LAYERS):
                n0 = L * LAYER_SLABS
                mix, mm, ffn = ("mix", L), ("mem", L), ("ffn", L)
                n = n0 + PHASE["qkv"]
                start(mix, n)

                def qk_free(G):
                    if not (isinstance(G, int) and G < 2):
                        pe.wait_ge(*LV(L, "qk_ev_a", G - 1))
                        pe.wait_ge(*LV(L, "qk_ev_d", G - 1))

                def qk_turn(G, par):
                    if L == 0:
                        pe.wait_ge(*LV(L, "rope", G * 10 + 10))
                    else:
                        pe.wait_ge(*LV(L, "qk_ev_a", G + 1))
                        pe.wait_ge(*LV(L, "qk_ev_d", G + 1))
                    if not (isinstance(G, int) and G == 0):
                        pe.wait_ge(*LV(L, "qk_st_a", G))
                        pe.wait_ge(*LV(L, "qk_st_d", G))
                    transposes(lambda j, h: tp[:, j // 2, (j % 2) * SEQ + h * P:(j % 2) * SEQ + (h + 1) * P],
                               lambda j, h: qk_stage[:, par, h, j * P:(j + 1) * P], 4, LS(L, "qk_t"))

                def qk_group(G, par, n):
                    qk_free(G)
                    for s in range(GS):
                        if s == 3:
                            qk_turn(G - 1, 1 - par)
                        slab(n + s, s % RING, par, SLAB_KT * s, KT, a_hi, a_lo)

                if L == 0:
                    pe.wait_ge(small_landed, 16 * 7)
                    pe.transpose(aux[:, 0, 0:P], gain_in[:], ident[:]).then_inc(sem("gain_t"), 1)
                qk_group(1, 1, n + GS)
                with pe.Fori(1, 4) as i:
                    for k in range(2):
                        qk_group(i * 2 + k, k, i * (2 * GS) + (n + k * GS))
                for vg in range(4):
                    if vg < 2:
                        qk_free(8 + vg)
                    else:
                        pe.wait_ge(*LV(L, "v_ev_a", vg - 1))
                        pe.wait_ge(*LV(L, "v_ev_d", vg - 1))
                    for s in range(GS):
                        if s == 3 and vg == 0:
                            qk_turn(7, 1)
                        if L and vg == 1 and s == 4:
                            pe.wait_ge(*LV(L, "wf_lo", 1))
                            o = aux[0:HEADS, 0, 0:SEQ]
                            for kt in range(KT):
                                pe.matmul(o, wf_hi[:, kt, :], a_hi[:, kt, :], start=(kt == 0), stop=False)
                                pe.matmul(o, wf_lo[:, kt, :], a_hi[:, kt, :], start=False, stop=False)
                                pe.matmul(o, wf_hi[:, kt, :], a_lo[:, kt, :], start=False, stop=(kt == KT - 1))
                            for h in range(HALF):
                                last = pe.matmul(aux[0:HEADS, 1, h * P:(h + 1) * P],
                                                 stat(1, h, h + 1).to_broadcast([P, HEADS]), ident[:],
                                                 start=True, stop=True)
                            last.then_inc(LS(L, "fg_mm"), 1)
                        slab(n + (8 + vg) * GS + s, s % RING, vg % 2, SLAB_KT * s, KT, a_hi, a_lo)
                        q = (vg - 1) * GS + s
                        if 0 <= q < 4 * D_GROUPS and q % 4 in (0, 1):
                            m = 2 * (q // 4) + q % 4
                            if q % 4 == 0:
                                pe.wait_ge(*LV(L, "mem_landed", 16 * (q // 4 + 1)))
                            if m == 0:
                                pe.wait_ge(*LV(L, "qk_st_a", 8))
                                pe.wait_ge(*LV(L, "qk_st_d", 8))
                            if m >= 2:
                                pe.wait_ge(*LV(L, "m_lo", SLAB_KT * (m - 1)))
                            transposes(lambda j, h: tp[:, m % 2, j * SEQ + h * P:j * SEQ + (h + 1) * P],
                                       lambda j, h: mem_in[:, h, (2 * (m % 2) + j) * P:(2 * (m % 2) + j + 1) * P],
                                       SLAB_KT, LS(L, "mem_t"))

                def slots(h):
                    if L:
                        return h, HEADS + h
                    q = (h // 8) * 16 + h % 8
                    return q, q + 8

                def scores(h):
                    q, k = slots(h)
                    if h == 0 and L:
                        pe.wait_ge(*LV(L, "fbias", 1))
                    if h >= 2:
                        pe.wait_ge(*LV(L, "s_max", 2 * (h - 1)))
                    for t, (a, b) in enumerate(((0, W0), (W0, W0 + W1))):
                        o = tp[:, h % 2, a:b]
                        last = pe.matmul(o, qkT[:, q, t * P:(t + 1) * P], qkT[:, k, 0:b - a], start=True, stop=(L == 0))
                        if L:
                            last = pe.matmul(o, sel[:, h:h + 1].to_broadcast([P // 2, P]), fb[:, 0:b - a],
                                             start=False, stop=True)
                    last.then_inc(LS(L, "s"), 1)

                def turn_probs(h):
                    pe.wait_ge(*LV(L, "p", 2 * (h + 1)))
                    if h >= 2:
                        pe.wait_ge(*LV(L, "p_st", h - 1))
                    for k in range(3):
                        last = pe.transpose(aux[:, h % 2, k * P:(k + 1) * P], prob[:, h % 4, k * P:(k + 1) * P], ident[:])
                    last.then_inc(LS(L, "p_t"), 1)

                def values(h):
                    pe.wait_ge(*LV(L, "p_st", h + 1))
                    if h == 0:
                        pe.wait_ge(*LV(L, "v_ev_a", 4))
                        pe.wait_ge(*LV(L, "v_ev_d", 4))
                    if h >= 2:
                        pe.wait_ge(*LV(L, "o_lo", h - 1))
                    o = acc[:, 1, h % 2, 0:SEQ]
                    cols = slice(h * P, (h + 1) * P)
                    pe.matmul(o, v_sb[:, 0, cols], probT[:, h % 2, 0:SEQ], start=True, stop=False)
                    pe.matmul(o[:, P:SEQ], v_sb[:, 1, cols], probT[:, h % 2, SEQ:SEQ + P], start=False, stop=True)\
                        .then_inc(LS(L, "o_t"), 1)

                n = n0 + PHASE["mk"]
                pe.wait_ge(*LV(L, "v_ev_a", 3))
                pe.wait_ge(*LV(L, "v_ev_d", 3))
                pe.wait_ge(*LV(L, "m_lo", KT))
                for s in range(GS):
                    for h in pair_heads(s):
                        scores(h)
                    for h in pair_heads(s - 2):
                        values(h)
                    slab(n + s, s % RING, 0, SLAB_KT * s, KT, m_hi, m_lo)
                    for h in pair_heads(s - 1):
                        turn_probs(h)

                def m_turn(k, src):
                    pe.wait_ge(*LV(L, "m_ev_a", 1 + k))
                    pe.wait_ge(*LV(L, "m_ev_d", 1 + k))
                    transposes(lambda j, h: aux[:, j // 2, (j % 2) * SEQ + h * P:(j % 2) * SEQ + (h + 1) * P],
                               lambda j, h: src[:, h, j * P:(j + 1) * P], 4, LS(L, "mqk_t"))

                n = n0 + PHASE["out"]
                for g in range(D_GROUPS):
                    y_free(mix, g)
                    for s in range(GS):
                        if g == 0:
                            for h in pair_heads(GS + s - 2):
                                values(h)
                            for h in pair_heads(GS + s - 1):
                                turn_probs(h)
                            if s == 0:
                                pe.wait_ge(*LV(L, "m_ev_a", 1))
                                pe.wait_ge(*LV(L, "m_ev_d", 1))
                            if s == 3:
                                pe.wait_ge(*LV(L, "p_st", HEADS))
                                m_turn(0, mk_stage)
                            if s == 5:
                                pe.wait_ge(*LV(L, "tables_landed", 96))
                                for t in range(CW + 1):
                                    last = pe.transpose(tp[:, 0, t * FF_TILES:(t + 1) * FF_TILES], conv_in[:, t, :],
                                                        ident[0:FF_TILES, 0:FF_TILES])
                                last.then_inc(LS(L, "conv_t"), 1)
                            pe.wait_ge(*LV(L, "o_lo", SLAB_KT * (s + 1)))
                        if g * GS + s >= D_GROUPS * GS - TAIL:
                            break
                        slab(n + g * GS + s, s % RING, g % 2, SLAB_KT * s, KT, a_hi, a_lo)
                n = n0 + PHASE["mq"]
                pe.wait_ge(*LV(L, "conv_st", 1))
                pe.wait_ge(*LV(L, "mqk_st_a", 1))
                pe.wait_ge(*LV(L, "mqk_st_d", 1))
                tail(mix, mm, n, KT, a_hi, a_lo)
                start(mm, n)

                def m_scores(h):
                    if h == 0:
                        for k in ("mqk_st_a", "mqk_st_d"):
                            pe.wait_ge(*LV(L, k, 2))
                    if h >= 2:
                        pe.wait_ge(*LV(L, "m_exp", 2 * (h - 1)))
                    for t in range(HALF):
                        last = pe.matmul(tp[:, h % 2, t * SEQ:(t + 1) * SEQ], mqT[:, h, t * P:(t + 1) * P], mkT[:, h, :],
                                         start=True, stop=True)
                    last.then_inc(LS(L, "ms"), 1)

                def m_turn_probs(h):
                    pe.wait_ge(*LV(L, "mp", 2 * (h + 1)))
                    if h >= 2:
                        pe.wait_ge(*LV(L, "mp_st", h - 1))
                    for t in range(HALF):
                        for b in range(HALF):
                            last = pe.transpose(aux[:, h % 2, b * SEQ + t * P:b * SEQ + (t + 1) * P],
                                                mprob[:, h, t * SEQ + b * P:t * SEQ + (b + 1) * P], ident[:])
                    last.then_inc(LS(L, "mp_t"), 1)

                n = n0 + PHASE["mv"]
                for s in range(GS):
                    if s == 1:
                        m_turn(1, mq_stage)
                    if 2 <= s < 2 + MEM_HEADS:
                        m_scores(s - 2)
                    if s < GS - 2:
                        if s >= 4:
                            m_turn_probs(s - 4)
                        slab(n + s, s % RING, 1, SLAB_KT * s, KT, m_hi, m_lo)
                for h in range(HALF):
                    for s in (GS - 2, GS - 1):
                        if s == GS - 2:
                            m_turn_probs(MEM_HEADS - 2 + h)
                        if h == 0:
                            pe.wait_ge(lo_ready, n + s + 1)
                        last = half_slab(h, s % RING, 1, SLAB_KT * s, KT, m_hi, m_lo)
                        if h:
                            last.then_inc(slab_used, 1)
                    if h == 0:
                        last.then_inc(LS(L, "mv_half"), 1)
                pe.wait_ge(*LV(L, "m_exp", 2 * MEM_HEADS))
                for b in range(HALF):
                    pe.wait_ge(*LV(L, ("m_ev_a", "m_ev_d")[b], 3))
                    for h in range(MEM_HEADS):
                        pe.wait_ge(*LV(L, "mp_st", h + 1))
                        last = pe.matmul(m_out(h), mv_sb[:, b, h * P:(h + 1) * P], mprobT[:, h, b * SEQ:(b + 1) * SEQ],
                                         start=(b == 0), stop=(b == 1))
                        if b:
                            last.then_inc(LS(L, "mo_t"), 1)
                n = n0 + PHASE["mo"]
                for g in range(2):
                    for s in range(MEM_GS):
                        k = g * MEM_GS + s
                        slab(n + k, k % RING, g % 2, SLAB_KT * s, MEM_KT, a_hi, a_lo,
                             LV(L, "mo_lo", SLAB_KT * s + 1))
                n = n0 + PHASE["up"]
                tail(mm, ffn, n, MEM_KT, a_hi, a_lo)
                start(ffn, n)

                def u_free(G):
                    if not (isinstance(G, int) and G < 2):
                        pe.wait_ge(*LV(L, "u_ev_a", G - 1))
                        pe.wait_ge(*LV(L, "u_ev_d", G - 1))

                def u_turn(G, src, dst):
                    pe.wait_ge(*LV(L, "u_ev_a", G + 1))
                    pe.wait_ge(*LV(L, "u_ev_d", G + 1))
                    if not (isinstance(G, int) and G < 2):
                        pe.wait_ge(*LV(L, "conv_done", (G - 1) * 8))
                    transposes(lambda j, h: dst[:, j // 2, (j % 2) * SEQ + h * P:(j % 2) * SEQ + (h + 1) * P],
                               lambda j, h: src[:, h, j * P:(j + 1) * P], 4, LS(L, "u_t"))

                def up_pair(i, n, first):
                    for q in range(GS if first else 0, 2 * GS):
                        if q % GS == 0:
                            u_free(i * 2 + q // GS)
                        if q == 2 and not first:
                            u_turn(i * 2 - 1, u_val, aux)
                        if q == GS + 2:
                            u_turn(i * 2, u_gate, tp)
                        slab(n + q, q % RING, q // GS, SLAB_KT * (q % GS), KT, a_hi, a_lo)

                up_pair(0, n, True)
                with pe.Fori(1, FF_GROUPS) as i:
                    up_pair(i, i * (2 * GS) + n, False)
                n = n0 + PHASE["down"]
                for g in range(D_GROUPS):
                    if g < 2:
                        u_free(2 * FF_GROUPS + g)
                    y_free(ffn, g)
                    for s in range(FF_GS):
                        if g == 0 and s == 2:
                            u_turn(2 * FF_GROUPS - 1, u_val, aux)
                        if g == 0:
                            pe.wait_ge(*LV(L, "hid_lo", (SLAB_KT * s) // 4 + 1))
                        k = g * FF_GS + s
                        if k >= D_GROUPS * FF_GS - TAIL:
                            break
                        slab(n + k, k % RING, g % 2, SLAB_KT * s, FF_KT, hid_hi, hid_lo)
                tail(ffn, ("mix", L + 1) if L + 1 < LAYERS else None, n + D_GROUPS * FF_GS, FF_KT, hid_hi, hid_lo)


def tables():
    inv_freq = np.float32(500000.0) ** (-np.arange(0, ROT, 2, dtype=np.float32) / np.float32(ROT))
    q = np.arange(SEQ)[:, None]
    k = np.arange(SEQ)[None, :]
    dist = q - k
    causal = dist >= 0
    seen = np.zeros((SEQ, SEQ), np.int64)
    for window, dil in ((128, 1), (512, 4), (2048, 16)):
        seen += causal & (dist % dil == 0) & (dist <= window)
    more = np.where(seen > 0, np.log(np.maximum(seen, 1)) / SCALE, MASKED)
    plain = np.where(causal, 0.0, MASKED)

    def pair(m):
        return np.concatenate([m[:P, :W0], m[P:, :W1]], axis=1).astype(np.float32)

    return (np.eye(P, dtype=np.float32), np.tile(inv_freq.astype(np.float32), (P, 1)), pair(plain), pair(more))


_INS = ["x", "mem", "positions", "w_in_ab", "w_out_ab", "w_in_c", "b_f", "w_out_c",
        "g_mix_pre", "g_mix_post", "g_mem_kv", "g_mem_pre", "g_mem_post",
        "w_mq", "w_mk", "w_mv", "w_mo", "g_ffn_pre", "g_ffn_post",
        "w_up", "conv_w", "conv_b", "w_down"]


def kernel(**inputs):
    import concourse.bacc as _bacc
    from concourse.bass_utils import run_bass_kernel_spmd as _run

    nc = _bacc.Bacc("TRN2", target_bir_lowering=False, num_devices=1)
    arrays, args = {}, []
    named = [(n, np.ascontiguousarray(inputs[n])) for n in _INS]
    named += list(zip(("identity", "inv_freq", "causal_mask", "dilated_mask"), tables()))
    for name, a in named:
        arrays[f"in_{name}"] = a
        args.append(nc.dram_tensor(f"in_{name}", a.shape, mybir.dt.from_np(a.dtype), kind="ExternalInput").ap())
    out = nc.dram_tensor("out_0", (1, SEQ, D), F32, kind="ExternalOutput").ap()
    build(nc, *args, out)
    r = _run(nc, [arrays], core_ids=[0])
    return r.results[0]["out_0"]
```
